# Optimizing a Trainium2 kernel written in Bass

```python
import jax
import jax.numpy as jnp
from jax import lax
import numpy as np
import math
import jax, jax.numpy as jnp

D_MODEL = 1024
BATCH = 1
SEQ = 512
DEPTH = 1

GRID_W = 64
CTX_LEN = 256
HG_HEADS = 4
HG_HEAD_DIM = 128
HG_WIDTH = HG_HEADS * HG_HEAD_DIM
DN_HEADS = 4
DN_HEAD_DIM = 128
DN_WIDTH = DN_HEADS * DN_HEAD_DIM
MIX_WIDTH = HG_WIDTH + DN_WIDTH
HG_CHUNK = 32
DN_CHUNK = 64
CONV_SIZE = 3
N_GROUPS = 4
EXPERTS_PER_GROUP = 4
N_EXPERTS = N_GROUPS * EXPERTS_PER_GROUP
TOP_K_IN_GROUP = 2
EXPERT_FF = 512
NORM_EPS = 1e-6
IN_SPLITS = [HG_WIDTH] * 5 + [DN_WIDTH] * 4 + [DN_HEADS] * 4
IN_COLS = sum(IN_SPLITS)


def rms_norm(x, w):
    x32 = x.astype(jnp.float32)
    y = x32 * lax.rsqrt(jnp.mean(x32 * x32, axis=-1, keepdims=True) + NORM_EPS)
    return (y * w.astype(jnp.float32)).astype(x.dtype)

def modulate(h, shift, scale):
    return h * (1 + scale) + shift

def l2_normalize(t):
    t32 = t.astype(jnp.float32)
    return (t32 * lax.rsqrt(jnp.sum(t32 * t32, axis=-1, keepdims=True) + NORM_EPS)).astype(t.dtype)

def to_heads(t, n_heads):
    b, length, width = t.shape
    return t.reshape(b, length, n_heads, width // n_heads).transpose(0, 2, 1, 3)

def gated_head_norm(o, gate, w):
    y = rms_norm(o, w) * jax.nn.silu(gate)
    b, h, length, d = y.shape
    return y.transpose(0, 2, 1, 3).reshape(b, length, h * d)

def split_in_proj(p):
    bounds = [int(v) for v in np.cumsum(IN_SPLITS)[:-1]]
    return jnp.split(p, bounds, axis=-1)

def gla_chunk_scan(q, k, v, log_f, s0):
    b, h, length, dk = q.shape
    dv = v.shape[-1]
    n = length // HG_CHUNK
    incl = jnp.tril(jnp.ones((HG_CHUNK, HG_CHUNK), dtype=bool))[:, :, None]

    def to_chunks(t):
        return jnp.moveaxis(t.reshape(b, h, n, HG_CHUNK, t.shape[-1]), 2, 0)

    def step(state, inp):
        qc, kc, vc, fc = inp
        cum = jnp.cumsum(fc, axis=2)
        diff = cum[:, :, :, None, :] - cum[:, :, None, :, :]
        decay = jnp.where(incl, jnp.exp(jnp.where(incl, diff, 0.0)), 0.0)
        attn = jnp.einsum('bhtd,bhsd,bhtsd->bhts', qc, kc, decay)
        o = jnp.einsum('bhtd,bhde->bhte', qc * jnp.exp(cum), state) + jnp.einsum('bhts,bhse->bhte', attn, vc)
        last = cum[:, :, -1, :]
        k_dec = kc * jnp.exp(last[:, :, None, :] - cum)
        state = jnp.exp(last)[..., None] * state + jnp.einsum('bhsd,bhse->bhde', k_dec, vc)
        return state, o

    state, o = lax.scan(step, s0, (to_chunks(q), to_chunks(k), to_chunks(v), to_chunks(log_f)))
    return jnp.moveaxis(o, 0, 2).reshape(b, h, length, dv), state

def gated_delta_chunk_scan(q, k, v, beta, log_a, s0):
    b, h, length, dk = q.shape
    dv = v.shape[-1]
    n = length // DN_CHUNK
    dt = q.dtype
    qn = q.reshape(b, h, n, DN_CHUNK, dk)
    kn = k.reshape(b, h, n, DN_CHUNK, dk)
    vn = v.reshape(b, h, n, DN_CHUNK, dv)
    bn = beta.reshape(b, h, n, DN_CHUNK).astype(jnp.float32)
    cum = jnp.cumsum(log_a.astype(jnp.float32).reshape(b, h, n, DN_CHUNK), axis=-1)
    incl = jnp.tril(jnp.ones((DN_CHUNK, DN_CHUNK), dtype=bool))
    strict = jnp.tril(jnp.ones((DN_CHUNK, DN_CHUNK), dtype=bool), -1)
    diff = cum[..., :, None] - cum[..., None, :]
    decay = jnp.where(incl, jnp.exp(jnp.where(incl, diff, 0.0)), 0.0)
    kk = jnp.einsum('bhntd,bhnsd->bhnts', kn, kn).astype(jnp.float32)
    a_mat = jnp.where(strict, bn[..., :, None] * kk * decay, 0.0) + jnp.eye(DN_CHUNK, dtype=jnp.float32)
    rhs = jnp.concatenate([kn.astype(jnp.float32) * (bn * jnp.exp(cum))[..., None],
                           vn.astype(jnp.float32) * bn[..., None]], axis=-1)
    sol = lax.linalg.triangular_solve(a_mat, rhs, left_side=True, lower=True, unit_diagonal=True)
    w = sol[..., :dk].astype(dt)
    u = sol[..., dk:].astype(dt)
    qk = jnp.einsum('bhntd,bhnsd->bhnts', qn, kn) * decay.astype(dt)
    q_dec = qn * jnp.exp(cum)[..., None].astype(dt)
    k_dec = kn * jnp.exp(cum[..., -1:] - cum)[..., None].astype(dt)
    g_tot = jnp.exp(cum[..., -1]).astype(dt)

    def step(state, inp):
        w_c, u_c, qk_c, qd_c, kd_c, gt_c = inp
        v_new = u_c - jnp.einsum('bhtd,bhde->bhte', w_c, state)
        o = jnp.einsum('bhtd,bhde->bhte', qd_c, state) + jnp.einsum('bhts,bhse->bhte', qk_c, v_new)
        state = gt_c[..., None, None] * state + jnp.einsum('bhtd,bhte->bhde', kd_c, v_new)
        return state, o

    xs = tuple(jnp.moveaxis(t, 2, 0) for t in (w, u, qk, q_dec, k_dec, g_tot))
    state, o = lax.scan(step, s0, xs)
    return jnp.moveaxis(o, 0, 2).reshape(b, h, length, dv), state

def run_bidirectional(scan_fn, ctx_fwd, lat_fwd, ctx_bwd, lat_bwd, s0):
    oc_f, sc_f = scan_fn(*ctx_fwd, s0)
    ox_f, _ = scan_fn(*lat_fwd, sc_f)
    oc_b, sc_b = scan_fn(*[jnp.flip(t, axis=2) for t in ctx_bwd], s0)
    ox_b, _ = scan_fn(*[jnp.flip(t, axis=2) for t in lat_bwd], sc_b)
    return oc_f + jnp.flip(oc_b, axis=2), ox_f + jnp.flip(ox_b, axis=2)

def hgrn2_log_forget(f_logit, lb):
    return jnp.logaddexp(jnp.log(lb), jnp.log1p(-lb) + jax.nn.log_sigmoid(f_logit))

def hgrn2_branch(cols_c, cols_x, lb, norm_w):
    def prep(cols):
        q, i, g, f_fwd, f_bwd = cols
        q = to_heads(jax.nn.silu(q), HG_HEADS)
        v = to_heads(i, HG_HEADS)
        per_dir = []
        for f_logit, lb_d in ((f_fwd, lb[0]), (f_bwd, lb[1])):
            log_f = to_heads(hgrn2_log_forget(f_logit, lb_d), HG_HEADS)
            per_dir.append((q, -jnp.expm1(log_f), v, log_f))
        return per_dir, to_heads(g, HG_HEADS)

    dirs_c, gc = prep(cols_c)
    dirs_x, gx = prep(cols_x)
    s0 = jnp.zeros((gc.shape[0], HG_HEADS, HG_HEAD_DIM, HG_HEAD_DIM), gc.dtype)
    oc, ox = run_bidirectional(gla_chunk_scan, dirs_c[0], dirs_x[0], dirs_c[1], dirs_x[1], s0)
    return gated_head_norm(oc, gc, norm_w), gated_head_norm(ox, gx, norm_w)

def short_conv_latent(t, w):
    b, length, ch = t.shape
    rows = length // GRID_W
    y = lax.conv_general_dilated(t.reshape(b, rows, GRID_W, ch), w[:, :, None, :], window_strides=(1, 1),
                                 padding='SAME', dimension_numbers=('NHWC', 'HWIO', 'NHWC'),
                                 feature_group_count=ch)
    return y.reshape(b, length, ch)

def short_conv_context(t, w):
    ch = t.shape[-1]
    return lax.conv_general_dilated(t, w[CONV_SIZE // 2][:, None, :], window_strides=(1,), padding='SAME',
                                    dimension_numbers=('NWC', 'WIO', 'NWC'), feature_group_count=ch)

def deltanet_branch(cols_c, cols_x, conv_w, a_log, dt_bias, norm_w):
    def prep(cols, conv_fn):
        q, k, v, z, b_fwd, b_bwd, a_fwd, a_bwd = cols
        qkv = jax.nn.silu(conv_fn(jnp.concatenate([q, k, v], axis=-1), conv_w))
        q, k, v = jnp.split(qkv, 3, axis=-1)
        q = l2_normalize(to_heads(q, DN_HEADS)) * (DN_HEAD_DIM ** -0.5)
        k = l2_normalize(to_heads(k, DN_HEADS))
        v = to_heads(v, DN_HEADS)
        per_dir = []
        for d, (b_logit, a_logit) in enumerate(((b_fwd, a_fwd), (b_bwd, a_bwd))):
            beta = jax.nn.sigmoid(b_logit).transpose(0, 2, 1)
            log_a = (-jnp.exp(a_log[d]) * jax.nn.softplus(a_logit + dt_bias[d])).transpose(0, 2, 1)
            per_dir.append((q, k, v, beta, log_a))
        return per_dir, to_heads(z, DN_HEADS)

    dirs_c, zc = prep(cols_c, short_conv_context)
    dirs_x, zx = prep(cols_x, short_conv_latent)
    s0 = jnp.zeros((zc.shape[0], DN_HEADS, DN_HEAD_DIM, DN_HEAD_DIM), zc.dtype)
    oc, ox = run_bidirectional(gated_delta_chunk_scan, dirs_c[0], dirs_x[0], dirs_c[1], dirs_x[1], s0)
    return gated_head_norm(oc, zc, norm_w), gated_head_norm(ox, zx, norm_w)

def hybrid_mixer(pc, px, lb, hg_norm_w, conv_w, a_log, dt_bias, dn_norm_w):
    cols_c = split_in_proj(pc)
    cols_x = split_in_proj(px)
    hg_c, hg_x = hgrn2_branch(cols_c[:5], cols_x[:5], lb, hg_norm_w)
    dn_c, dn_x = deltanet_branch(cols_c[5:], cols_x[5:], conv_w, a_log, dt_bias, dn_norm_w)
    return jnp.concatenate([hg_c, dn_c], axis=-1), jnp.concatenate([hg_x, dn_x], axis=-1)

def hierarchical_moe(h, w_group, b_group, w_expert, b_expert, w_gate, w_up, w_down):
    t = h.reshape(-1, h.shape[-1])
    g_logits = (t @ w_group + b_group).astype(jnp.float32)
    g_prob = jax.nn.softmax(g_logits, axis=-1)
    g_idx = jnp.argmax(g_logits, axis=-1)
    g_w = jnp.take_along_axis(g_prob, g_idx[:, None], axis=-1)
    e_logits = (t @ w_expert + b_expert).astype(jnp.float32).reshape(-1, N_GROUPS, EXPERTS_PER_GROUP)
    e_in_group = jnp.take_along_axis(e_logits, g_idx[:, None, None], axis=1)[:, 0]
    top_v, top_i = lax.top_k(e_in_group, TOP_K_IN_GROUP)
    top_w = jax.nn.softmax(top_v, axis=-1) * g_w
    expert_id = g_idx[:, None] * EXPERTS_PER_GROUP + top_i
    gates = jnp.sum(jax.nn.one_hot(expert_id, N_EXPERTS, dtype=jnp.float32) * top_w[..., None],
                    axis=1).astype(t.dtype)
    y = jnp.zeros_like(t)
    for e in range(N_EXPERTS):
        a = jax.nn.silu(t @ w_gate[e]) * (t @ w_up[e])
        y = y + gates[:, e:e + 1] * (a @ w_down[e])
    return y.reshape(h.shape)

def first_inputs(seed: int = 0) -> dict:
    key = jax.random.key(seed)
    ks = jax.random.split(key, 24)
    f32 = jnp.float32

    def nrm(k, shape, scale):
        return jax.random.normal(k, shape, f32) * scale

    a_init = jax.random.uniform(ks[13], (DEPTH, 2, DN_HEADS), f32, minval=1.0, maxval=16.0)
    dt = jnp.exp(jax.random.uniform(ks[14], (DEPTH, 2, DN_HEADS), f32,
                                    minval=float(np.log(1e-3)), maxval=float(np.log(1e-1))))
    return {
        'x': nrm(ks[0], (BATCH, SEQ, D_MODEL), 1.0),
        'c': nrm(ks[1], (BATCH, D_MODEL), 1.0),
        'ctx': nrm(ks[2], (BATCH, CTX_LEN, D_MODEL), 1.0),
        'c_ctx': nrm(ks[3], (D_MODEL,), 1.0),
        'w_mod': nrm(ks[4], (DEPTH, D_MODEL, 6 * D_MODEL), 0.5 * D_MODEL ** -0.5),
        'b_mod': nrm(ks[5], (DEPTH, 6 * D_MODEL), 0.02),
        'norm1_w': 1.0 + nrm(ks[6], (DEPTH, D_MODEL), 0.02),
        'norm2_w': 1.0 + nrm(ks[7], (DEPTH, D_MODEL), 0.02),
        'w_in': nrm(ks[8], (DEPTH, D_MODEL, IN_COLS), D_MODEL ** -0.5),
        'w_out': nrm(ks[9], (DEPTH, MIX_WIDTH, D_MODEL), MIX_WIDTH ** -0.5),
        'hg_lb': nrm(ks[10], (DEPTH, 2, HG_WIDTH), 0.1),
        'hg_norm_w': 1.0 + nrm(ks[11], (DEPTH, HG_HEAD_DIM), 0.02),
        'dn_conv_w': nrm(ks[12], (DEPTH, CONV_SIZE, CONV_SIZE, 3 * DN_WIDTH), 1.0 / CONV_SIZE),
        'dn_a_log': jnp.log(a_init),
        'dn_dt_bias': dt + jnp.log(-jnp.expm1(-dt)),
        'dn_norm_w': 1.0 + nrm(ks[15], (DEPTH, DN_HEAD_DIM), 0.02),
        'w_group': nrm(ks[16], (DEPTH, D_MODEL, N_GROUPS), D_MODEL ** -0.5),
        'b_group': nrm(ks[17], (DEPTH, N_GROUPS), 0.01),
        'w_expert': nrm(ks[18], (DEPTH, D_MODEL, N_EXPERTS), D_MODEL ** -0.5),
        'b_expert': nrm(ks[19], (DEPTH, N_EXPERTS), 0.01),
        'w_gate': nrm(ks[20], (DEPTH, N_EXPERTS, D_MODEL, EXPERT_FF), D_MODEL ** -0.5),
        'w_up': nrm(ks[21], (DEPTH, N_EXPERTS, D_MODEL, EXPERT_FF), D_MODEL ** -0.5),
        'w_down': nrm(ks[22], (DEPTH, N_EXPERTS, EXPERT_FF, D_MODEL), EXPERT_FF ** -0.5),
        'final_norm_w': 1.0 + nrm(ks[23], (D_MODEL,), 0.02),
    }

def first_block(x, c, ctx, c_ctx, w_mod, b_mod, norm1_w, norm2_w, w_in, w_out, hg_lb, hg_norm_w,
              dn_conv_w, dn_a_log, dn_dt_bias, dn_norm_w, w_group, b_group, w_expert, b_expert,
              w_gate, w_up, w_down, final_norm_w):
    lb_all = jnp.cumsum(jax.nn.softmax(hg_lb.astype(jnp.float32), axis=0), axis=0)
    lb_all = (lb_all - lb_all[0]).astype(x.dtype)
    silu_c = jax.nn.silu(c)
    silu_c_ctx = jax.nn.silu(c_ctx)
    xs, cs = x, ctx
    for l in range(DEPTH):
        last = l == DEPTH - 1
        sh1x, sc1x, g1x, sh2x, sc2x, g2x = jnp.split((silu_c @ w_mod[l] + b_mod[l])[:, None, :], 6, axis=-1)
        sh1c, sc1c, g1c, sh2c, sc2c, g2c = jnp.split((silu_c_ctx @ w_mod[l] + b_mod[l])[None, None, :], 6, axis=-1)
        hx = modulate(rms_norm(xs, norm1_w[l]), sh1x, sc1x)
        hc = modulate(rms_norm(cs, norm1_w[l]), sh1c, sc1c)
        oc, ox = hybrid_mixer(hc @ w_in[l], hx @ w_in[l], lb_all[l], hg_norm_w[l], dn_conv_w[l],
                              dn_a_log[l], dn_dt_bias[l], dn_norm_w[l])
        moe_args = (w_group[l], b_group[l], w_expert[l], b_expert[l], w_gate[l], w_up[l], w_down[l])
        xs = xs + g1x * (ox @ w_out[l])
        xs = xs + g2x * hierarchical_moe(modulate(rms_norm(xs, norm2_w[l]), sh2x, sc2x), *moe_args)
        if not last:
            cs = cs + g1c * (oc @ w_out[l])
            cs = cs + g2c * hierarchical_moe(modulate(rms_norm(cs, norm2_w[l]), sh2c, sc2c), *moe_args)
    return rms_norm(xs, final_norm_w)


DEPTH_2 = 2

HEAD_DIM = 64
ROPE_THETA = 10000.0
Q_BLOCK = 128
EPS = 1e-6
N_MOD = 6
DIFF_HEADS = 4
DIFF_QK_DIM = HEAD_DIM
DIFF_V_DIM = 2 * HEAD_DIM
GQA_Q_HEADS = 8
GQA_KV_HEADS = 2
GQA_GROUP = GQA_Q_HEADS // GQA_KV_HEADS
ATTN_IN = DIFF_HEADS * (4 * DIFF_QK_DIM + DIFF_V_DIM) + (GQA_Q_HEADS + 2 * GQA_KV_HEADS) * HEAD_DIM
ATTN_OUT = DIFF_HEADS * DIFF_V_DIM + GQA_Q_HEADS * HEAD_DIM
SGU_DIM = D_MODEL
SGU_GROUPS = 4
SGU_CHUNK = 128
FFN_DIM = 2816
CONV_W = 3
N_EVEN = (DEPTH_2 + 1) // 2
N_ODD = DEPTH_2 // 2


def rms_norm_2(x, g):
    xf = x.astype(jnp.float32)
    y = xf * lax.rsqrt(jnp.mean(xf * xf, axis=-1, keepdims=True) + EPS)
    return (y * g.astype(jnp.float32)).astype(x.dtype)

def modulate_2(h, shift, scale):
    return h * (1 + scale) + shift

def axial_rope_tables(rows):
    n_freq = HEAD_DIM // 4
    inv = ROPE_THETA ** (-jnp.arange(n_freq, dtype=jnp.float32) / n_freq)
    row = jnp.repeat(jnp.arange(rows, dtype=jnp.float32), GRID_W)
    col = jnp.tile(jnp.arange(GRID_W, dtype=jnp.float32), rows)
    ang = jnp.concatenate([row[:, None] * inv, col[:, None] * inv], axis=-1)
    return jnp.cos(ang), jnp.sin(ang)

def apply_rope(x, cos, sin):
    xf = x.astype(jnp.float32).reshape(x.shape[:-1] + (x.shape[-1] // 2, 2))
    x0, x1 = xf[..., 0], xf[..., 1]
    c = cos[None, :, None, :]
    s = sin[None, :, None, :]
    out = jnp.stack([x0 * c - x1 * s, x0 * s + x1 * c], axis=-1).reshape(x.shape)
    return out.astype(x.dtype)

def attn_project(h, w_in, q_norm, k_norm, rope):
    B, S, _ = h.shape
    qk_a = DIFF_HEADS * DIFF_QK_DIM
    sizes = [qk_a, qk_a, qk_a, qk_a, DIFF_HEADS * DIFF_V_DIM,
             GQA_Q_HEADS * HEAD_DIM, GQA_KV_HEADS * HEAD_DIM, GQA_KV_HEADS * HEAD_DIM]
    splits = [int(v) for v in np.cumsum(sizes)[:-1]]
    q1, q2, k1, k2, va, qb, kb, vb = jnp.split(h @ w_in, splits, axis=-1)
    heads = lambda t, n: t.reshape(B, S, n, -1)
    q1, q2, k1, k2, va = (heads(t, DIFF_HEADS) for t in (q1, q2, k1, k2, va))
    qb = rms_norm_2(heads(qb, GQA_Q_HEADS), q_norm)
    kb = rms_norm_2(heads(kb, GQA_KV_HEADS), k_norm)
    vb = heads(vb, GQA_KV_HEADS)
    if rope is not None:
        cos, sin = rope
        q1, q2, k1, k2, qb, kb = (apply_rope(t, cos, sin) for t in (q1, q2, k1, k2, qb, kb))
    return q1, q2, qb, k1, k2, va, kb, vb

def diff_attend(q1, q2, k1, k2, v, lam):
    scale = DIFF_QK_DIM ** -0.5
    p1 = jax.nn.softmax(jnp.einsum('bqhd,bkhd->bhqk', q1, k1).astype(jnp.float32) * scale, axis=-1)
    p2 = jax.nn.softmax(jnp.einsum('bqhd,bkhd->bhqk', q2, k2).astype(jnp.float32) * scale, axis=-1)
    p = (p1 - lam * p2).astype(v.dtype)
    return jnp.einsum('bhqk,bkhv->bqhv', p, v)

def gqa_attend(q, k, v):
    B, Q, H, d = q.shape
    qg = q.reshape(B, Q, GQA_KV_HEADS, GQA_GROUP, d)
    s = jnp.einsum('bqgrd,bkgd->bgrqk', qg, k).astype(jnp.float32) * (d ** -0.5)
    p = jax.nn.softmax(s, axis=-1).astype(v.dtype)
    return jnp.einsum('bgrqk,bkgd->bqgrd', p, v).reshape(B, Q, H, d)

def attn_heads(q1, q2, qb, k1, k2, va, kb, vb, lam, lam_init, subln):
    B, Q = q1.shape[:2]
    oa = rms_norm_2(diff_attend(q1, q2, k1, k2, va, lam), subln) * (1 - lam_init)
    ob = gqa_attend(qb, kb, vb)
    return jnp.concatenate([oa.reshape(B, Q, -1), ob.reshape(B, Q, -1)], axis=-1)

def sweep_query_blocks(fn, qs):
    B, S = qs[0].shape[:2]
    nb = S // Q_BLOCK
    blocks = tuple(jnp.moveaxis(q.reshape((B, nb, Q_BLOCK) + q.shape[2:]), 1, 0) for q in qs)
    out = lax.map(lambda qb: fn(*qb), blocks)
    return jnp.moveaxis(out, 0, 1).reshape(B, S, out.shape[-1])

def attention_mixer(h_lat, h_ctx, w_in, w_out, lq1, lk1, lq2, lk2, subln, q_norm, k_norm,
                    lam_init, rope, with_ctx_out):
    lat = attn_project(h_lat, w_in, q_norm, k_norm, rope)
    ctx = attn_project(h_ctx, w_in, q_norm, k_norm, None)
    lam = (jnp.exp(jnp.sum(lq1.astype(jnp.float32) * lk1.astype(jnp.float32)))
           - jnp.exp(jnp.sum(lq2.astype(jnp.float32) * lk2.astype(jnp.float32))) + lam_init)
    K1, K2, VA, KB, VB = (jnp.concatenate([ctx[i], lat[i]], axis=1) for i in range(3, 8))
    lat_fn = lambda q1b, q2b, qbb: attn_heads(q1b, q2b, qbb, K1, K2, VA, KB, VB, lam, lam_init, subln)
    y_lat = sweep_query_blocks(lat_fn, lat[:3]) @ w_out
    y_ctx = None
    if with_ctx_out:
        y_ctx = attn_heads(*ctx, lam, lam_init, subln) @ w_out
    return y_lat, y_ctx

def sgu_mixer(h, w_in, v_norm, w_s, b_s, w_out):
    B, S, _ = h.shape
    z = jax.nn.gelu(h @ w_in, approximate=False)
    u, v = jnp.split(z, 2, axis=-1)
    v = rms_norm_2(v, v_norm)
    n = S // SGU_CHUNK
    vg = v.reshape(B, n, SGU_CHUNK, SGU_GROUPS, SGU_DIM // SGU_GROUPS)
    mixed = jnp.einsum('gpq,bnqgc->bnpgc', w_s, vg) + b_s.T[:, :, None]
    return (u * mixed.reshape(B, S, SGU_DIM)) @ w_out

def conv_ffn(h, w_up, conv_w, conv_b, w_down):
    S = h.shape[1]
    z = h @ w_up
    zp = jnp.pad(z, ((0, 0), (1, 1), (0, 0)))
    z = conv_w[0] * zp[:, :S] + conv_w[1] * zp[:, 1:S + 1] + conv_w[2] * zp[:, 2:] + conv_b
    g, u = jnp.split(z, 2, axis=-1)
    return (jax.nn.silu(g) * u) @ w_down

def second_inputs(seed: int = 0) -> dict:
    key = jax.random.key(seed)
    ks = iter(jax.random.split(key, 32))
    D = D_MODEL
    nrm = lambda shape, s: jax.random.normal(next(ks), shape, jnp.float32) * s
    return {
        "x": nrm((BATCH, SEQ, D), 1.0),
        "c": nrm((BATCH, D), 1.0),
        "ctx": nrm((BATCH, CTX_LEN, D), 1.0),
        "c_ctx": nrm((D,), 1.0),
        "ada_w": nrm((DEPTH_2, D, N_MOD * D), 0.5 * D ** -0.5),
        "ada_b": nrm((DEPTH_2, N_MOD * D), 0.02),
        "mix_norm": 1.0 + nrm((DEPTH_2, D), 0.1),
        "ffn_norm": 1.0 + nrm((DEPTH_2, D), 0.1),
        "final_norm": 1.0 + nrm((D,), 0.1),
        "attn_w_in": nrm((N_EVEN, D, ATTN_IN), D ** -0.5),
        "attn_w_out": nrm((N_EVEN, ATTN_OUT, D), ATTN_OUT ** -0.5),
        "diff_lq1": nrm((N_EVEN, DIFF_QK_DIM), 0.1),
        "diff_lk1": nrm((N_EVEN, DIFF_QK_DIM), 0.1),
        "diff_lq2": nrm((N_EVEN, DIFF_QK_DIM), 0.1),
        "diff_lk2": nrm((N_EVEN, DIFF_QK_DIM), 0.1),
        "diff_subln": 1.0 + nrm((N_EVEN, DIFF_V_DIM), 0.1),
        "gqa_q_norm": 1.0 + nrm((N_EVEN, HEAD_DIM), 0.1),
        "gqa_k_norm": 1.0 + nrm((N_EVEN, HEAD_DIM), 0.1),
        "sgu_w_in": nrm((N_ODD, D, 2 * SGU_DIM), D ** -0.5),
        "sgu_v_norm": 1.0 + nrm((N_ODD, SGU_DIM), 0.1),
        "sgu_w_s": nrm((N_ODD, SGU_GROUPS, SGU_CHUNK, SGU_CHUNK), SGU_CHUNK ** -0.5),
        "sgu_b_s": 1.0 + nrm((N_ODD, SGU_GROUPS, SGU_CHUNK), 0.1),
        "sgu_w_out": nrm((N_ODD, SGU_DIM, D), SGU_DIM ** -0.5),
        "ffn_w_up": nrm((DEPTH_2, D, 2 * FFN_DIM), D ** -0.5),
        "ffn_conv_w": nrm((DEPTH_2, CONV_W, 2 * FFN_DIM), CONV_W ** -0.5),
        "ffn_conv_b": nrm((DEPTH_2, 2 * FFN_DIM), 0.02),
        "ffn_w_down": nrm((DEPTH_2, FFN_DIM, D), FFN_DIM ** -0.5),
    }

def second_block(x, c, ctx, c_ctx, ada_w, ada_b, mix_norm, ffn_norm, final_norm,
              attn_w_in, attn_w_out, diff_lq1, diff_lk1, diff_lq2, diff_lk2, diff_subln,
              gqa_q_norm, gqa_k_norm, sgu_w_in, sgu_v_norm, sgu_w_s, sgu_b_s, sgu_w_out,
              ffn_w_up, ffn_conv_w, ffn_conv_b, ffn_w_down):
    rows = x.shape[1] // GRID_W
    rope = axial_rope_tables(rows)
    last_attn = (DEPTH_2 - 1) // 2 * 2
    s_c = jax.nn.silu(c)
    s_cc = jax.nn.silu(c_ctx)
    for l in range(DEPTH_2):
        i = l // 2
        is_attn = l % 2 == 0
        update_ctx = l < last_attn
        m_lat = (s_c @ ada_w[l] + ada_b[l])[:, None, :]
        sh1, sc1, g1, sh2, sc2, g2 = jnp.split(m_lat, N_MOD, axis=-1)
        h_lat = modulate_2(rms_norm_2(x, mix_norm[l]), sh1, sc1)
        if is_attn or update_ctx:
            m_ctx = s_cc @ ada_w[l] + ada_b[l]
            csh1, csc1, cg1, csh2, csc2, cg2 = jnp.split(m_ctx, N_MOD, axis=-1)
            h_ctx = modulate_2(rms_norm_2(ctx, mix_norm[l]), csh1, csc1)
        if is_attn:
            lam_init = 0.8 - 0.6 * math.exp(-0.3 * l)
            y_lat, y_ctx = attention_mixer(h_lat, h_ctx, attn_w_in[i], attn_w_out[i],
                                           diff_lq1[i], diff_lk1[i], diff_lq2[i], diff_lk2[i],
                                           diff_subln[i], gqa_q_norm[i], gqa_k_norm[i],
                                           lam_init, rope, update_ctx)
        else:
            y_lat = sgu_mixer(h_lat, sgu_w_in[i], sgu_v_norm[i], sgu_w_s[i], sgu_b_s[i], sgu_w_out[i])
            if update_ctx:
                y_ctx = sgu_mixer(h_ctx, sgu_w_in[i], sgu_v_norm[i], sgu_w_s[i], sgu_b_s[i], sgu_w_out[i])
        x = x + g1 * y_lat
        x = x + g2 * conv_ffn(modulate_2(rms_norm_2(x, ffn_norm[l]), sh2, sc2),
                              ffn_w_up[l], ffn_conv_w[l], ffn_conv_b[l], ffn_w_down[l])
        if update_ctx:
            ctx = ctx + cg1 * y_ctx
            ctx = ctx + cg2 * conv_ffn(modulate_2(rms_norm_2(ctx, ffn_norm[l]), csh2, csc2),
                                       ffn_w_up[l], ffn_conv_w[l], ffn_conv_b[l], ffn_w_down[l])
    return rms_norm_2(x, final_norm)


def setup_inputs(seed=0):
    out = dict(first_inputs(seed))
    for name, value in second_inputs(seed + 1).items():
        if name != "x":
            out[name + "_2"] = value
    return out


def reference(
    x, c, ctx, c_ctx, w_mod, b_mod, norm1_w, norm2_w, w_in, w_out, hg_lb, hg_norm_w, dn_conv_w,
    dn_a_log, dn_dt_bias, dn_norm_w, w_group, b_group, w_expert, b_expert, w_gate, w_up, w_down,
    final_norm_w, c_2, ctx_2, c_ctx_2, ada_w_2, ada_b_2, mix_norm_2, ffn_norm_2, final_norm_2,
    attn_w_in_2, attn_w_out_2, diff_lq1_2, diff_lk1_2, diff_lq2_2, diff_lk2_2, diff_subln_2,
    gqa_q_norm_2, gqa_k_norm_2, sgu_w_in_2, sgu_v_norm_2, sgu_w_s_2, sgu_b_s_2, sgu_w_out_2,
    ffn_w_up_2, ffn_conv_w_2, ffn_conv_b_2, ffn_w_down_2,
):
    x = first_block(
        x, c, ctx, c_ctx, w_mod, b_mod, norm1_w, norm2_w, w_in, w_out, hg_lb, hg_norm_w,
        dn_conv_w, dn_a_log, dn_dt_bias, dn_norm_w, w_group, b_group, w_expert, b_expert,
        w_gate, w_up, w_down, final_norm_w,
    )
    return second_block(
        x, c_2, ctx_2, c_ctx_2, ada_w_2, ada_b_2, mix_norm_2, ffn_norm_2, final_norm_2,
        attn_w_in_2, attn_w_out_2, diff_lq1_2, diff_lk1_2, diff_lq2_2, diff_lk2_2, diff_subln_2,
        gqa_q_norm_2, gqa_k_norm_2, sgu_w_in_2, sgu_v_norm_2, sgu_w_s_2, sgu_b_s_2, sgu_w_out_2,
        ffn_w_up_2, ffn_conv_w_2, ffn_conv_b_2, ffn_w_down_2,
    )


_drawn_inputs = setup_inputs


def setup_inputs(seed=0):
    import zlib

    import numpy as np

    out = dict(_drawn_inputs(seed))
    spreads = {}
    factors = {'ctx': 3.984,
     'c_ctx': 6.634,
     'norm1_w': 7.722,
     'norm2_w': 6.238,
     'hg_norm_w': 8.0,
     'dn_norm_w': 8.0,
     'b_group': 8.0,
     'b_expert': 29.238,
     'final_norm_w': 2.741,
     'diff_lq1_2': 22.328,
     'diff_lq2_2': 3.477,
     'diff_lk2_2': 2.988,
     'diff_subln_2': 13.068,
     'gqa_q_norm_2': 8.0,
     'gqa_k_norm_2': 8.0,
     'sgu_b_s_2': 7.483,
     'ffn_conv_b_2': 19.026,
     'ffn_norm_2': 3.804,
     'diff_lk1_2': 8.0,
     'sgu_v_norm_2': 6.918}
    for name, (base, spread) in spreads.items():
        noise = np.random.default_rng([zlib.crc32(name.encode()), seed]).standard_normal(out[name].shape)
        drawn = base * np.exp(spread * noise) if base else spread * noise
        out[name] = jnp.asarray(drawn.astype(out[name].dtype))
    for name, factor in factors.items():
        out[name] = (out[name] * factor).astype(out[name].dtype)
    return out
```

```python
from contextlib import ExitStack

import concourse.bass as bass
from concourse import mybir

F32 = mybir.dt.float32
U32 = mybir.dt.uint32
ALU = mybir.AluOpType
ACT = mybir.ActivationFunctionType
X = mybir.AxisListType.X

P = 128
D = 1024
KD = D // P
SEQ = 512
CTX = 256
TOK = CTX + SEQ
NC = TOK // P
NX = SEQ // P
NCC = CTX // P
BANK = 512
RING = 6
SLOT = 2048
CW = SLOT // KD
EPS = 1e-6
HEADS = 4
LEVELS = 7
GRID_W = 64
GRID_R = SEQ // GRID_W
N_EXP = 16
FF = 512
FFN = 2816
NF = FFN // P
KV = 1280


def build(nc, ins, out, stop=None, dbg=None, skip=()):
    ctx = ExitStack()
    with ctx:
        def sb(name, shape, dt=F32):
            return ctx.enter_context(nc.sbuf_tensor(name, shape, dt))

        class Sems(dict):
            def __missing__(self, name):
                self[name] = ctx.enter_context(nc.semaphore(name))
                return self[name]

        s = Sems()

        xres = sb("xres", [P, NX, D])
        ring = sb("ring", [P, RING, SLOT])
        hT = sb("hT", [P, KD, SEQ])
        hcT = sb("hcT", [P, KD, CTX])
        cols = sb("cols", [P, 7, P])
        levm = sb("levm", [P, LEVELS, 2, P])
        cmask = sb("cmask", [P, 4, P])
        ident = sb("ident", [P, P])
        ones = sb("ones", [P, P])
        gate = sb("gate", [P, 2, D])
        modc = sb("modc", [P, 4 * KD, 2])
        mcol = sb("mcol", [P, 2, 2, KD])
        silc = sb("silc", [P, KD, 2])
        stat = sb("stat", [P, 64])
        etab = sb("etab", [P, 24], mybir.dt.int32)
        thr = sb("thr", [P, 4])
        wba = sb("wba", [P, KD, 16])
        hgw = sb("hgw", [P, 2, P])
        aldt = sb("aldt", [P, 2, 8])
        ARENA = 24064
        arena = sb("arena", [P, ARENA])
        ps = ctx.enter_context(nc.psum_tensor("ps", [P, 8, BANK], F32))

        def at(off, *shape):
            n = 1
            for k in shape:
                n *= k
            assert off + n <= ARENA, (off, shape)
            v = arena[:, off:off + n]
            names = "abcdef"[:len(shape)]
            if len(shape) == 1:
                return v
            return v.rearrange(f"p ({' '.join(names)}) -> p {' '.join(names)}",
                               **{k: m for k, m in zip(names, shape)})

        class Place:
            def __init__(self, off=0):
                self.off = off

            def __call__(self, *shape):
                v = at(self.off, *shape)
                for_n = 1
                for k in shape:
                    for_n *= k
                self.off += for_n
                return v

        def bc(ap, shape, axis):
            return ap.unsqueeze(axis).broadcast_to(shape)

        class Stream:
            def __init__(self, eng):
                self.eng, self.n, self.i, self.per = eng, 0, 0, 0
                self.owed = False

            def loop(self, i, per):
                assert per % RING == 0
                self.i, self.per, self.start = i, per, self.n

            def end(self, times):
                assert self.n - self.start == self.per
                self.n = self.start + times * self.per
                self.i = self.per = 0

            def load(self, src, width=SLOT):
                n = self.n
                if n >= RING:
                    self.eng.wait_ge(s["chunk_used"], self.i * self.per + (n - RING + 1))
                slot = ring[:, n % RING, 0:width]
                a = src.shape[1]
                self.eng.dma_start(slot.rearrange("p (a b) -> p a b", a=a), src).then_inc(s[f"chunk_in{n % RING}"], 16)
                self.n += 1

            def take(self, a, width=SLOT):
                n = self.n
                self.eng.wait_ge(s[f"chunk_in{n % RING}"], self.i * (self.per // RING * 16) + 16 * (n // RING + 1))
                self.n += 1
                return ring[:, n % RING, 0:width].rearrange("p (a b) -> p a b", a=a)

            def done(self):
                assert not self.owed
                self.owed = True

            def pay(self, step=None):
                if self.owed:
                    (step if step is not None else self.eng.drain()).then_inc(s["chunk_used"], 1)
                    self.owed = False

        class Chain:
            def __init__(self, eng, name):
                self.eng, self.sem, self.n, self.base = eng, s[name], 0, 0

            def mark(self, step):
                step.then_inc(self.sem, 1)
                self.n += 1
                return self.n

            def wait(self, n=None):
                self.eng.wait_ge(self.sem, self.base + (self.n if n is None else n))

            def link(self, step):
                self.mark(step)
                self.wait()

            def loop(self, i, per):
                self.base, self.per, self.start = i * per, per, self.n

            def end(self, times):
                assert self.n - self.start == self.per, (self.n - self.start, self.per)
                self.n = self.start + times * self.per
                self.base = 0

        meetings = {}

        def meet(eng, who):
            k = meetings[who] = meetings.get(who, 0) + 1
            eng.drain().then_inc(s["stage_done"], 1)
            eng.wait_ge(s["stage_done"], 4 * k)

        w_in = ins["w_in"][0].rearrange("(k p) n -> p k n", p=P)

        def cols_of(w, c0, n=CW):
            return w[:, :, c0:c0 + n]

        HGQ, HGI, HGG, HGF, HGB, DNQ, DNK, DNV, DNZ = (512 * j for j in range(9))

        STAGES = ["consts", "mod1", "norm1", "hg0", "hg1", "dn0", "dn1", "wout", "moe", "mod2", "norm2", "proj", "rope", "attn", "awout", "ffn0", "mod3", "norm3", "sgu", "sguout", "ffn1", "final"]
        upto = len(STAGES) if stop is None else STAGES.index(stop) + 1

        def on(name):
            return STAGES.index(name) < upto and name not in skip

        MOE = int(on("moe"))

        rows = at(0, 7, P)
        brow = at(7 * P, 2 * D)
        ROWS = [(0, 0, ins["c"].rearrange("a (k p) -> (a k) p", p=P)),
                (0, 8, ins["c_ctx"].rearrange("(k p) -> k p", p=P)),
                (0, 16, ins["c_2"].rearrange("a (k p) -> (a k) p", p=P)),
                (0, 24, ins["c_ctx_2"].rearrange("(k p) -> k p", p=P)),
                (0, 32, ins["norm1_w"].rearrange("a (k p) -> (a k) p", p=P)),
                (0, 40, ins["norm2_w"].rearrange("a (k p) -> (a k) p", p=P)),
                (0, 48, ins["mix_norm_2"].rearrange("a (k p) -> (a k) p", p=P)),
                (0, 64, ins["ffn_norm_2"].rearrange("a (k p) -> (a k) p", p=P)),
                (0, 80, ins["b_mod"].rearrange("a (k p) -> (a k) p", p=P)),
                (1, 0, ins["ada_b_2"].rearrange("a (k p) -> (a k) p", p=P)),
                (1, 96, ins["sgu_b_s_2"].rearrange("a g p -> (a g) p")),
                (2, 0, ins["dn_conv_w"].rearrange("l a b (k p) -> (l a b k) p", p=P))]
        for l in range(2):
            cw = ins["ffn_conv_w_2"][l].rearrange("a (k p) -> (a k) p", p=P)
            ROWS += [(3 + 2 * l, 0, cw[0:4 * NF, :]), (4 + 2 * l, 0, cw[4 * NF:6 * NF, :]),
                     (4 + 2 * l, 2 * NF, ins["ffn_conv_b_2"][l:l + 1, :].rearrange("a (k p) -> (a k) p", p=P))]
        NROW = [128, 100, 108, 88, 88, 88, 88]

        def col(t, r, n=1):
            return cols[:, t, r:r + n]

        MODB = [(0, 80), (1, 0), (1, 48)]

        def sp_consts(sp):
            for t, r, src in ROWS:
                sp.dma_start(rows[r:r + src.shape[0], t, :], src).then_inc(s["rows_in"], 16)
            sp.dma_start(aldt[:, 0, :], ins["dn_a_log"].rearrange("l d h -> l (d h)").broadcast_to([P, 8])).then_inc(s["rows_in"], 16)
            sp.dma_start(aldt[:, 1, :], ins["dn_dt_bias"].rearrange("l d h -> l (d h)").broadcast_to([P, 8])).then_inc(s["rows_in"], 16)
            sp.dma_start(hgw[:, 0, :], ins["hg_norm_w"].broadcast_to([P, P])).then_inc(s["rows_in"], 16)
            sp.dma_start(hgw[:, 1, :], ins["dn_norm_w"].broadcast_to([P, P])).then_inc(s["rows_in"], 16)
            sp.dma_start(wba[:, :, :], cols_of(w_in, 4608, 16)).then_inc(s["rows_in"], 16)
        N_ROWS_IN = 16 * (len(ROWS) + 5)

        def pool_consts(g, ch):
            ch.mark(g.memset(ident[:, :], 0.0))
            ch.mark(g.memset(ones[:, :], 1.0))
            for k in range(SEQ // P):
                g.memset(thr[:, k:k + 1], float(P * k))
            ch.mark(g.memset(cmask[:, :, :], 1.0))
            ch.link(g.memset(levm[:, :, :, :], 0.0))
            g.affine_select(out=ident[:, :], in_=ident[:, :], compare_op=ALU.not_equal, fill=1.0, base=0,
                            pattern=[[-1, P]], channel_multiplier=1).then_inc(s["ident_ready"], 1)
            for j, (cm, st, b, op) in enumerate([(-1, 1, 0, ALU.is_ge), (1, -1, 0, ALU.is_ge),
                                                 (1, -1, 0, ALU.is_gt), (-1, 1, 0, ALU.is_gt)]):
                g.affine_select(out=cmask[:, j, :], in_=cmask[:, j, :], compare_op=op, fill=0.0, base=b,
                                pattern=[[st, P]], channel_multiplier=cm)
            for l in range(LEVELS):
                h = 1 << l
                nb = P // (2 * h)
                for d in range(2):
                    v = levm[:, l, d, :].rearrange("p (n two h) -> p n two h", two=2, h=h)[:, :, 1 - d, :]
                    lo = h * d
                    ch.link(g.memset(v, 1.0))
                    ch.link(g.affine_select(out=v, in_=v, compare_op=ALU.is_ge, fill=0.0, base=-lo,
                                            pattern=[[-2 * h, nb], [0, h]], channel_multiplier=1))
                    g.affine_select(out=v, in_=v, compare_op=ALU.is_ge, fill=0.0, base=lo + h - 1,
                                    pattern=[[2 * h, nb], [0, h]], channel_multiplier=-1)

        def pe_consts(pe):
            pe.wait_ge(s["ident_ready"], 1)
            pe.wait_ge(s["rows_in"], N_ROWS_IN)
            for t, n in enumerate(NROW):
                last = pe.transpose(ps[:, t // 4, (t % 4) * P:(t % 4) * P + n], rows[0:n, t, :], ident[0:n, 0:n])
            last.then_inc(s["cols_ps"], 1)

        def dve_consts(v):
            v.wait_ge(s["cols_ps"], 1)
            for t, n in enumerate(NROW):
                v.tensor_copy(cols[:, t, 0:n], ps[:, t // 4, (t % 4) * P:(t % 4) * P + n])

        MODW = [ins["w_mod"][0], ins["ada_w_2"][0], ins["ada_w_2"][1]]
        MODBV = [ins["b_mod"][0:1, :], ins["ada_b_2"][0:1, :], ins["ada_b_2"][1:2, :]]
        crep = at(7 * P + 2 * D, KD, P)

        def sp_mod(sp, W, j):
            w = MODW[j].rearrange("(k p) n -> p k n", p=P)
            for q in range(6 * D // CW):
                W.load(cols_of(w, q * CW))

        def act_mod(a, ch, j):
            for q, sec in enumerate((2, 5)):
                a.dma_start(brow[0:1, q * D:(q + 1) * D], MODBV[j][:, sec * D:(sec + 1) * D]).then_inc(s["brow_in"], 16)
            c0 = 0 if j == 0 else 16
            src = cols[:, 0, c0:c0 + 16].rearrange("p (two k) -> p k two", two=2)
            ch.link(a.activation(silc[:, :, :], src, ACT.Silu))
            a.activation(crep[:, :, :], bc(silc[:, :, 0], [P, KD, P], 2), ACT.Copy).then_inc(s["silc_ready"], 1)

        def pe_mod(pe, W, j):
            pe.wait_ge(s["silc_ready"], j + 1)
            pe.wait_ge(s["brow_in"], 32 * (j + 1))
            for q in range(6 * D // CW):
                w = W.take(KD)
                sec, part = divmod(q, D // CW)
                if sec in (2, 5):
                    g = 0 if sec == 2 else 1
                    o = ps[:, 1 + 2 * g + part // 2, (part % 2) * CW:(part % 2 + 1) * CW]
                    for k in range(KD):
                        pe.matmul(o, crep[:, k, :], w[:, k, :], start=(k == 0), stop=False)
                    last = pe.matmul(o, ones[0:1, :], brow[0:1, g * D + part * CW:g * D + (part + 1) * CW],
                                     start=False, stop=True)
                else:
                    sc = {0: 0, 1: 1, 3: 2, 4: 3}[sec]
                    for c in range(CW // P):
                        t = sc * KD + part * (CW // P) + c
                        for k in range(KD):
                            last = pe.matmul(ps[:, 0, 2 * t:2 * t + 2], w[:, k, c * P:(c + 1) * P], silc[:, k, :],
                                             start=(k == 0), stop=(k == KD - 1))
                last.then_inc(s["chunk_used"], 1)
            pe.drain().then_inc(s["mod_ps"], 1)
        def mod_used(j):
            return 24 * (j + 1)

        def dve_mod(v, ch, j, normcols, upto_chunks):
            v.wait_ge(s["mod_ps"], upto_chunks)
            t, r = MODB[j]
            for q, sec in enumerate((0, 1, 3, 4)):
                n = ch.mark(v.tensor_tensor(modc[:, q * KD:(q + 1) * KD, :],
                                            ps[:, 0, 2 * q * KD:2 * (q + 1) * KD].rearrange("p (a b) -> p a b", b=2),
                                            bc(col(t, r + sec * KD, KD), [P, KD, 2], 2), ALU.add))
            ch.wait()
            for q in range(2):
                sc = modc[:, (2 * q + 1) * KD:(2 * q + 2) * KD, :].rearrange("p k two -> p two k")
                ch.link(v.tensor_scalar(mcol[:, q, :, :], sc, 1.0, None, ALU.add))
                ch.mark(v.tensor_tensor(mcol[:, q, :, :], mcol[:, q, :, :], bc(normcols[q], [P, 2, KD], 1), ALU.mult))
            for g in range(2):
                v.tensor_copy(gate[:, g, :].rearrange("p (a b) -> p a b", a=2), ps[:, 1 + 2 * g:3 + 2 * g, :])

        nidx = {"act": 0, "dve": 0, "pe": 0}

        def act_norm(a, x, T, junk, dst, which, cx, xn, ss, shift0):
            n = nidx["act"] = nidx["act"] + 1
            for m in range(T):
                last = a.activation(xn[:, m, :], x[:, m, :], ACT.Square, accum_out=ss[:, m:m + 1])
            last.then_inc(s["sumsq"], 1)
            a.wait_ge(s["mean_ready"], n)
            a.activation(ss[:, 0:T], ss[:, 0:T], ACT.Sqrt).then_inc(s["root"], 1)
            if dst is None:
                return
            for k in range(1, KD, 2):
                a.wait_ge(s["xnT_ps"], KD * tcount["act"] + k + 1)
                a.activation(dst[:, k, :], ps[:, k, 0:T * P], ACT.Identity,
                             bias=modc[:, shift0 + k, cx:cx + 1], scale=mcol[:, which, cx, k:k + 1])
            tcount["act"] += 1

        tcount = {"act": 0, "dve": 0, "pe": 0}

        def dve_norm(v, ch, x, T, dst, which, cx, xn, ss, shift0):
            n = nidx["dve"] = nidx["dve"] + 1
            v.wait_ge(s["sumsq"], n)
            v.tensor_scalar(ss[:, 0:T], ss[:, 0:T], 1.0 / D, EPS, ALU.mult, ALU.add).then_inc(s["mean_ready"], 1)
            v.wait_ge(s["root"], n)
            ch.link(v.reciprocal(ss[:, 0:T], ss[:, 0:T]))
            for m in range(T):
                last = v.tensor_scalar(xn[:, m, :], x[:, m, :], ss[:, m:m + 1], None, ALU.mult)
            last.then_inc(s["xn_ready"], 1)
            if dst is None:
                return
            for k in range(0, KD, 2):
                v.wait_ge(s["xnT_ps"], KD * tcount["dve"] + k + 1)
                v.tensor_scalar(dst[:, k, :], ps[:, k, 0:T * P], mcol[:, which, cx, k:k + 1],
                                modc[:, shift0 + k, cx:cx + 1], ALU.mult, ALU.add)
            tcount["dve"] += 1

        def pe_norm(pe, T, xn):
            n = nidx["pe"] = nidx["pe"] + 1
            pe.wait_ge(s["xn_ready"], n)
            for k in range(KD):
                for m in range(T):
                    last = pe.transpose(ps[:, k, m * P:(m + 1) * P], xn[:, m, k * P:(k + 1) * P], ident[:, :])
                last.then_inc(s["xnT_ps"], 1)

        cres = at(8192, NCC, D)
        xn_buf = at(0, NX, D)
        njunk = at(12288, D)

        o_sb = at(0, NX, D)
        gz = xres

        pl = Place(NX * D)
        hv = pl(NC, 2, P)
        hq = pl(2, SEQ)
        hP = pl(2, 2, TOK)
        hK = pl(2, 2, TOK)
        hQ = pl(2, TOK)
        qt = [pl(2, SEQ) for _ in range(2)]
        kt = [pl(2, SEQ) for _ in range(2)]
        hA = pl(NX, 2, P)
        hS = pl(5, 2, 2, P)
        hE = pl(2, 2, NC)
        kd = at(pl.off - 0, 1)
        kd = arena[:, NX * D + 1536 + 1024 + 3072 + 3072 + 1536:][:, 0:3072].rearrange(
            "p (d c h x) -> p d c h x", d=2, c=NC, h=2)
        ORDER = [[0, 1, 2, 3, 4, 5], [1, 0, 5, 4, 3, 2]]
        HU = 20

        def sp_hg(sp, W, p):
            for c0 in (HGI, HGQ, HGG, HGF, HGB):
                W.load(cols_of(w_in, c0 + p * CW))

        def hg_units():
            u = [("v", m) for m in range(NC)] + [("q", j) for j in range(2)] + [("g", m) for m in range(NX)]
            for d in range(2):
                u += [("f", (d, j, part)) for j in range(2) for part in range(2)]
            return u

        def pe_proj(pe, W, units, name, total, p):
            w = None
            for u, (kind, idx, newchunk, endchunk) in enumerate(units):
                if newchunk:
                    w = W.take(KD)
                if u >= 8:
                    pe.wait_ge(s[name + "_out"], total * p + u - 7)
                b = u % 8
                if kind in "vgz":
                    hsrc, m = (hcT, idx) if (kind == "v" and idx < NCC) else (hT, idx - NCC if kind == "v" else idx)
                    for k in range(KD):
                        last = pe.matmul(ps[:, b, 0:CW], hsrc[:, k, m * P:(m + 1) * P], w[:, k, :],
                                         start=(k == 0), stop=(k == KD - 1))
                        if k == 0:
                            W.pay(last)
                else:
                    j, part = idx
                    src, n = (hcT, CTX) if part == 0 else (hT, SEQ)
                    for k in range(KD):
                        last = pe.matmul(ps[:, b, 0:n], w[:, k, j * P:(j + 1) * P], src[:, k, :],
                                         start=(k == 0), stop=(k == KD - 1))
                        if k == 0:
                            W.pay(last)
                last.then_inc(s[name + "_ps"], 1)
                if endchunk:
                    W.done()
            W.pay()

        HG_UNITS = ([("v", m, m == 0, m == NC - 1) for m in range(NC)]
                    + [("q", (j, 1), j == 0, j == 1) for j in range(2)]
                    + [("g", m, m == 0, m == NX - 1) for m in range(NX)]
                    + [("f", (j, part), (j, part) == (0, 0), (j, part) == (1, 1))
                       for d in range(2) for j in range(2) for part in range(2)])
        assert len(HG_UNITS) == HU

        def pe_hg(pe, W, p):
            pe_proj(pe, W, HG_UNITS, "hgp", HU, p)
            pe.wait_ge(s["hgp_out"], HU * (p + 1))
            for u in range(15):
                pe.wait_ge(s["qt_ready"], 15 * p + u + 1)
                if u:
                    pe.wait_ge(s["kt_ready"], 14 * p + u)
                if u >= 2:
                    pe.wait_ge(s["scores_out"], 15 * p + u - 1)
                q = hq if u == 0 else qt[u % 2]
                for c in range(NX):
                    for h in range(2):
                        last = pe.matmul(ps[:, 2 * (u % 2) + c // 2, ((c % 2) * 2 + h) * P:((c % 2) * 2 + h + 1) * P],
                                         kt[u % 2][:, h, c * P:(c + 1) * P], q[:, h, c * P:(c + 1) * P],
                                         start=True, stop=True)
                last.then_inc(s["scores_ps"], 1)
            pe.wait_ge(s["scores_out"], 15 * (p + 1))
            pe.wait_ge(s["kdec_ready"], 2 * (p + 1))
            for n in range(24):
                d, r = divmod(n, 12)
                c, h = divmod(r, 2)
                last = pe.transpose(ps[:, 2 + n // 4, (n % 4) * P:(n % 4 + 1) * P], hK[:, d, h, c * P:(c + 1) * P], ident[:, :])
            last.then_inc(s["kd_ps"], 1)
            pe.wait_ge(s["kd_ready"], p + 1)
            for k in range(5):
                for d in range(2):
                    c = ORDER[d][k]
                    for h in range(2):
                        last = pe.matmul(ps[:, k, (2 * d + h) * P:(2 * d + h + 1) * P], kd[:, d, c, h, :], hv[:, c, h, :],
                                         start=True, stop=True)
            last.then_inc(s["hadd_ps"], 1)
            pe.wait_ge(s["hS_ready"], p + 1)
            pe.wait_ge(s["qdec_ready"], 2 * (p + 1))
            for c in range(NX):
                for h in range(2):
                    o = ps[:, 5 + c // 2, ((c % 2) * 2 + h) * P:((c % 2) * 2 + h + 1) * P]
                    pe.matmul(o, hA[:, c, h, :], hv[:, NCC + c, h, :], start=True, stop=False)
                    pe.matmul(o, hP[:, 0, h, CTX + c * P:CTX + (c + 1) * P], hS[:, 1 + c, 0, h, :], start=False, stop=False)
                    last = pe.matmul(o, hP[:, 1, h, CTX + c * P:CTX + (c + 1) * P], hS[:, 4 - c, 1, h, :],
                                     start=False, stop=True)
            last.then_inc(s["ho_ps"], 1)

        def act_hg(a, p):
            for u, (kind, idx, _, _) in enumerate(HG_UNITS):
                a.wait_ge(s["hgp_ps"], HU * p + u + 1)
                b = u % 8
                if kind == "v":
                    last = a.activation(hv[:, idx, :, :], ps[:, b, 0:CW].rearrange("p (a b) -> p a b", a=2), ACT.Copy)
                elif kind == "q":
                    last = a.activation(hq[:, idx[0], :], ps[:, b, :], ACT.Silu)
                elif kind == "g":
                    last = a.activation(gz[:, idx, p * CW:(p + 1) * CW], ps[:, b, 0:CW], ACT.Silu)
                else:
                    j, part = idx
                    d = (u - 12) // 4
                    t0, n = (0, CTX) if part == 0 else (CTX, SEQ)
                    a.activation(hP[:, d, j, t0:t0 + n], ps[:, b, 0:n], ACT.Sigmoid)
                    last = a.activation(hK[:, d, j, t0:t0 + n], ps[:, b, 0:n], ACT.Sigmoid, scale=-1.0)
                last.then_inc(s["hgp_out"], 1)
            a.wait_ge(s["kd_ps"], p + 1)
            for n in range(6):
                last = a.activation(kd.rearrange("p d c h x -> p (d c h x)")[:, n * BANK:(n + 1) * BANK], ps[:, 2 + n, :], ACT.Copy)
            last.then_inc(s["kd_ready"], 1)

        def halves(v, h):
            w = v.rearrange("p a (n two h) -> p a n two h", two=2, h=h)
            return w[:, :, :, 0, :], w[:, :, :, 1, :]

        def flat_halves(v, h):
            w = v.rearrange("p a (n two h) -> p (a n) two h", two=2, h=h)
            return w[:, :, 0, :], w[:, :, 1, :]

        def pool_hg(g, ch, p):
            g.wait_ge(s["hgp_out"], HU * (p + 1))
            for d in range(2):
                if d:
                    g.wait_ge(s["kdec_ready"], 2 * p + 1)
                ch.link(g.memset(hQ[:, :, :], 1.0))
                for l in range(LEVELS):
                    u = 1 + d * LEVELS + l
                    h = 1 << l
                    if u >= 2:
                        g.wait_ge(s["scores_ps"], 15 * p + u - 1)
                    else:
                        g.wait_ge(s["kt_clear"], p + 1)
                    side = d
                    dst = halves(kt[u % 2], h)[side]
                    g.tensor_tensor(dst, halves(hK[:, d, :, CTX:], h)[side], halves(hQ[:, :, CTX:], h)[side],
                                    ALU.mult).then_inc(s["kt_ready"], 1)
                    g.wait_ge(s["kt_ready"], 14 * p + u)
                    if l:
                        g.wait_ge(s["P_grown"], 14 * p + d * LEVELS + l)
                    mine, other = flat_halves(hQ, h)[side], flat_halves(hP[:, d], h)[1 - side]
                    e = h - 1 if d == 0 else 0
                    n = 2 * TOK // (2 * h)
                    ch.link(g.tensor_tensor(mine, mine, other[:, :, e:e + 1].broadcast_to([P, n, h]), ALU.mult))
                    g.sem_inc(s["Q_grown"], 1)
                g.wait_ge(s["kt_ready"], 14 * p + (d + 1) * LEVELS)
                g.tensor_tensor(hK[:, d, :, :], hK[:, d, :, :], hQ[:, :, :], ALU.mult).then_inc(s["kdec_ready"], 1)

        def dve_hg(v, ch, p):
            if p == 0:
                for b in range(2):
                    ch.mark(v.memset(qt[b][:, :, :], 0.0))
                ch.mark(v.memset(kt[1][:, :, :], 0.0))
            ch.link(v.memset(hA[:, :, :, :], 0.0))
            v.wait_ge(s["hgp_out"], HU * (p + 1))
            v.tensor_tensor(kt[0][:, :, :], hK[:, 0, :, CTX:], hK[:, 1, :, CTX:], ALU.add).then_inc(s["qt_ready"], 1)
            v.sem_inc(s["kt_clear"], 1)

            def scores_out(u):
                v.wait_ge(s["scores_ps"], 15 * p + u + 1)
                for b in range(2):
                    m = ident[:, :] if u == 0 else levm[:, (u - 1) % LEVELS, (u - 1) // LEVELS, :]
                    last = v.copy_predicated(hA[:, 2 * b:2 * b + 2, :, :].rearrange("p a b c -> p (a b) c"),
                                             bc(m.bitcast(U32), [P, 4, P], 1),
                                             ps[:, 2 * (u % 2) + b, :].rearrange("p (a c) -> p a c", c=P))
                last.then_inc(s["scores_out"], 1)

            grown = None
            for d in range(2):
                for l in range(LEVELS):
                    u = 1 + d * LEVELS + l
                    h = 1 << l
                    if grown:
                        ch.wait(grown)
                    if u >= 3:
                        v.wait_ge(s["scores_ps"], 15 * p + u - 1)
                    side = 1 - d
                    v.tensor_tensor(halves(qt[u % 2], h)[side], halves(hq, h)[side],
                                    halves(hP[:, d, :, CTX:], h)[side], ALU.mult).then_inc(s["qt_ready"], 1)
                    scores_out(u - 1)
                    v.wait_ge(s["Q_grown"], 14 * p + d * LEVELS + l + 1)
                    v.wait_ge(s["qt_ready"], 15 * p + u + 1)
                    mine, other = flat_halves(hP[:, d], h)[side], flat_halves(hP[:, d], h)[1 - side]
                    e = h - 1 if d == 0 else 0
                    n = 2 * TOK // (2 * h)
                    grown = ch.mark(v.tensor_tensor(mine, mine, other[:, :, e:e + 1].broadcast_to([P, n, h]), ALU.mult))
                    ch.wait()
                    v.sem_inc(s["P_grown"], 1)
                ch.link(v.tensor_copy(hE[:, d, :, :], hP[:, d].rearrange("p a (c t) -> p a c t", t=P)[:, :, :, P - 1 if d == 0 else 0]))
                v.tensor_tensor(hP[:, d, :, CTX:], hP[:, d, :, CTX:], hq[:, :, :], ALU.mult).then_inc(s["qdec_ready"], 1)
            scores_out(14)
            v.wait_ge(s["hadd_ps"], p + 1)
            ch.link(v.tensor_copy(hS[:, 0].rearrange("p a b c -> p (a b c)"), ps[:, 0, :]))
            for k in range(1, 5):
                for d in range(2):
                    for h in range(2):
                        ch.mark(v.scalar_tensor_tensor(out=hS[:, k, d, h, :], in0=hS[:, k - 1, d, h, :],
                                                       scalar=hE[:, d, h, ORDER[d][k]:ORDER[d][k] + 1],
                                                       in1=ps[:, k, (2 * d + h) * P:(2 * d + h + 1) * P],
                                                       op0=ALU.mult, op1=ALU.add))
                ch.wait()
            v.sem_inc(s["hS_ready"], 1)
            v.wait_ge(s["ho_ps"], p + 1)
            for b in range(2):
                v.tensor_copy(o_sb[:, 2 * b:2 * b + 2, p * CW:(p + 1) * CW],
                              ps[:, 5 + b, :].rearrange("p (a c) -> p a c", a=2))

        pl = Place(NX * D)
        R1 = pl.off
        pq, pkv = pl(2, SEQ), pl(4, TOK)
        R2 = pl.off
        cq, ckv = pl(2, SEQ), pl(4, TOK)
        XT = pl(NC, 4, P)
        XI = pl(NC, 4, P)
        AT = pl(NC, 4, P)
        dA = pl(NX, 4, P)
        mr = arena[:, R2 + 2560:R2 + 2560 + 512].rearrange("p (d h x) -> p d h x", d=2, h=2)
        dec = arena[:, R2 + 3072:R2 + 3584].rearrange("p (d h x) -> p d h x", d=2, h=2)
        al = [pl(4, P), arena[:, R2 + 3584:R2 + 4096].rearrange("p (a x) -> p a x", a=4)]
        Mb = [mr.rearrange("p d h x -> p (d h) x"), dec.rearrange("p d h x -> p (d h) x")]
        tq = arena[:, R1:R1 + 1024].rearrange("p (c h x) -> p c h x", c=NX, h=2)
        tk = arena[:, R1 + 1024:R1 + 2560].rearrange("p (c h x) -> p c h x", c=NC, h=2)
        tv = arena[:, R1 + 2560:R1 + 4096].rearrange("p (c h x) -> p c h x", c=NC, h=2)
        QT = arena[:, R2:R2 + 1024].rearrange("p (c h x) -> p c h x", c=NX, h=2)
        KT = arena[:, R2 + 1024:R2 + 2560].rearrange("p (c h x) -> p c h x", c=NC, h=2)
        sq = XT
        dU = XI
        dS = AT
        zb = al[0]
        kx = [al[1], Mb[0]]
        dss = stat[:, 0:20]
        bet = sb("bet", [P, NC, 8])
        lga = sb("lga", [P, NC, 8])
        dex = sb("dex", [P, 3, NC, 8])
        nex = sb("nex", [P, NC, 8])
        dtmp = sb("dtmp", [P, 3, NC, 8])

        DN_UNITS = ([("q", (j, 1), j == 0, j == 1) for j in range(2)]
                    + [("kv", (j, part), (j, part) == (0, 0), (j, part) == (1, 1))
                       for t in range(2) for j in range(2) for part in range(2)]
                    + [("z", m, m == 0, m == NX - 1) for m in range(NX)])
        DU = len(DN_UNITS)

        def sp_dn(sp, W, p):
            for c0 in (DNQ, DNK, DNV, DNZ):
                W.load(cols_of(w_in, c0 + p * CW))

        def pe_dn(pe, W, p):
            pe_proj(pe, W, DN_UNITS, "dnp", DU, p)
            if p == 0:
                pe.wait_ge(s["dnp_out"], DU)
                for c in range(NC):
                    src, m = (hcT, c) if c < NCC else (hT, c - NCC)
                    for k in range(KD):
                        last = pe.matmul(ps[:, 7, c * 16:(c + 1) * 16], src[:, k, m * P:(m + 1) * P], wba[:, k, :],
                                         start=(k == 0), stop=(k == KD - 1))
                last.then_inc(s["ba_ps"], 1)
                pe.wait_ge(s["lga_ready"], 1)
                for d in range(2):
                    rhs = lga[:, :, 4 * d:4 * d + 4]
                    for q in range(2):
                        pe.matmul(ps[:, 6, (q * 2 + d) * 24:(q * 2 + d + 1) * 24], cmask[:, 2 * q + d, :], rhs, start=True, stop=True)
                pe.matmul(ps[:, 6, 96:144], ones[:, :], lga[:, :, :], start=True, stop=True).then_inc(s["dex_ps"], 1)
                pe.wait_ge(s["dex_ready"], 1)
            pe.wait_ge(s["conv_done"], p + 1)
            n = 0
            for src, cnt, c0 in ((cq, NX, 0), (ckv[:, 0:2, :], NC, 0), (ckv[:, 2:4, :], NC, 0)):
                for c in range(cnt):
                    for h in range(2):
                        last = pe.transpose(ps[:, n // 4, (n % 4) * P:(n % 4 + 1) * P], src[:, h, c * P:(c + 1) * P], ident[:, :])
                        n += 1
            last.then_inc(s["tok_ps"], 1)
            pe.wait_ge(s["tok_out"], 2 * (p + 1))
            pe.wait_ge(s["qk_normed"], p + 1)
            n = 0
            for src, cnt in ((tq, NX), (tk, NC)):
                for c in range(cnt):
                    for h in range(2):
                        last = pe.transpose(ps[:, n // 4, (n % 4) * P:(n % 4 + 1) * P], src[:, c, h, :], ident[:, :])
                        n += 1
            last.then_inc(s["chan_ps"], 1)
            pe.wait_ge(s["chan_ready"], p + 1)
            for c in range(NC):
                b = 2 * (c % 2)
                if c >= 2:
                    pe.wait_ge(s["sys_out"], NC * p + c - 1)
                for h in range(2):
                    last = pe.matmul(ps[:, b + 1, h * P:(h + 1) * P], KT[:, c, h, :], KT[:, c, h, :], start=True, stop=True)
                    if c >= NCC:
                        pe.matmul(ps[:, b + 1, (2 + h) * P:(3 + h) * P], KT[:, c, h, :], QT[:, c - NCC, h, :], start=True, stop=True)
                pe.wait_ge(s["mr_ready"], NC * p + c + 1)
                for d in range(2):
                    last = pe.matmul(ps[:, b, 2 * d * P:2 * (d + 1) * P], cmask[:, 2 + d, :],
                                     mr[:, d].rearrange("p h x -> p (h x)"), start=True, stop=True)
                last.then_inc(s["sys_ps"], 1)
            pe.wait_ge(s["sys_out"], NC * (p + 1))
            for c in range(NC):
                b = 4 + c % 2
                pe.wait_ge(s["al_ready"], NC * LEVELS * p + c + 1)
                if c >= 2:
                    pe.wait_ge(s["inv_out"], NC * LEVELS * p + c - 1)
                for a in range(4):
                    last = pe.transpose(ps[:, b, a * P:(a + 1) * P], al[c % 2][:, a, :], ident[:, :])
                last.then_inc(s["inv_ps"], 1)
            U0 = NC * LEVELS * p

            def products(u):
                c = u % NC
                pe.wait_ge(s["al_ready"], U0 + u + 1)
                pe.wait_ge(s["inv_out"], U0 + u - NC + 1)
                if u >= NC + 2:
                    pe.wait_ge(s["M_ready"], NC * (LEVELS - 1) * p + u - NC - 1)
                for a in range(4):
                    last = pe.matmul(ps[:, u % 2, a * P:(a + 1) * P], al[u % 2][:, a, :], XI[:, c, a, :], start=True, stop=True)
                last.then_inc(s["M_ps"], 1)

            def corrections(u):
                c = u % NC
                pe.wait_ge(s["M_ready"], NC * (LEVELS - 1) * p + u - NC + 1)
                pe.wait_ge(s["inv_out"], U0 + u - 1)
                m = Mb[u % 2]
                for a in range(4):
                    if u // NC < LEVELS - 1:
                        pe.matmul(ps[:, 2 + u % 2, a * P:(a + 1) * P], XT[:, c, a, :], m[:, a, :], start=True, stop=True)
                    last = pe.matmul(ps[:, 4 + u % 2, a * P:(a + 1) * P], m[:, a, :], XT[:, c, a, :], start=True, stop=True)
                last.then_inc(s["inv_ps"], 1)

            products(NC)
            for u in range(NC, NC * LEVELS):
                if u + 1 < NC * LEVELS:
                    products(u + 1)
                corrections(u)
            pe.wait_ge(s["inv_out"], U0 + NC * LEVELS)
            for k in range(NC):
                if k:
                    pe.wait_ge(s["dS_ready"], (NC - 1) * p + k)
                    for d in range(2):
                        c = ORDER[d][k]
                        for h in range(2):
                            a = 2 * d + h
                            last = pe.matmul(ps[:, 0, a * P:(a + 1) * P], KT[:, c, h, :], dS[:, k - 1, a, :], start=True, stop=True)
                    last.then_inc(s["ks_ps"], 1)
                    pe.wait_ge(s["z_ready"], (NC - 1) * p + k)
                for d in range(2):
                    c = ORDER[d][k]
                    for h in range(2):
                        a = 2 * d + h
                        last = pe.matmul(ps[:, 1, a * P:(a + 1) * P], XT[:, c, a, :], tv[:, c, h, :] if k == 0 else zb[:, a, :],
                                         start=True, stop=True)
                last.then_inc(s["u_ps"], 1)
                pe.wait_ge(s["u_ready"], NC * p + k + 1)
                if k < NC - 1:
                    pe.wait_ge(s["kx_ready"], (NC - 1) * p + k + 1)
                    for d in range(2):
                        c = ORDER[d][k]
                        for h in range(2):
                            a = 2 * d + h
                            last = pe.matmul(ps[:, 2, a * P:(a + 1) * P], kx[k % 2][:, a, :], dU[:, c, a, :], start=True, stop=True)
                    last.then_inc(s["add_ps"], 1)
            for c in range(NX):
                b = 3 + 2 * (c % 2)
                if c >= 2:
                    pe.wait_ge(s["do_out"], NX * p + c - 1)
                for h in range(2):
                    for d in range(2):
                        a = 2 * d + h
                        pe.matmul(ps[:, b, a * P:(a + 1) * P], QT[:, c, h, :], dS[:, 1 + c if d == 0 else 4 - c, a, :], start=True, stop=True)
                        last = pe.matmul(ps[:, b + 1, h * P:(h + 1) * P], dA[:, c, a, :], dU[:, NCC + c, a, :],
                                         start=(d == 0), stop=(d == 1))
                last.then_inc(s["do_ps"], 1)

        def act_dn(a, ch, p):
            for u, (kind, idx, _, _) in enumerate(DN_UNITS):
                a.wait_ge(s["dnp_ps"], DU * p + u + 1)
                b = u % 8
                if kind == "q":
                    last = a.activation(pq[:, idx[0], :], ps[:, b, :], ACT.Copy)
                elif kind == "kv":
                    j, part = idx
                    t = (u - 2) // 4
                    t0, n = (0, CTX) if part == 0 else (CTX, SEQ)
                    last = a.activation(pkv[:, 2 * t + j, t0:t0 + n], ps[:, b, 0:n], ACT.Copy)
                else:
                    last = a.activation(gz[:, idx, 512 + p * CW:512 + (p + 1) * CW], ps[:, b, 0:CW], ACT.Silu)
                last.then_inc(s["dnp_out"], 1)
            if p == 0:
                a.wait_ge(s["ba_ps"], 1)
                ba = ps[:, 7, 0:96].rearrange("p (c x) -> p c x", x=16)
                a.activation(bet[:, :, :], ba[:, :, 0:8], ACT.Sigmoid).then_inc(s["bet_ready"], 1)
                a.wait_ge(s["dt_added"], 1)
                ch.link(a.activation(dtmp[:, 1], dtmp[:, 0], ACT.Abs))
                ch.link(a.activation(dtmp[:, 1], dtmp[:, 1], ACT.Exp, scale=-1.0))
                ch.mark(a.activation(aldt[:, 0, :], aldt[:, 0, :], ACT.Exp))
                a.activation(dtmp[:, 1], dtmp[:, 1], ACT.Ln, bias=ones[:, 0:1]).then_inc(s["soft_ready"], 1)
                a.wait_ge(s["dex_ps"], 1)
                for d in range(2):
                    for q in range(2):
                        a.activation(dex[:, q, :, 4 * d:4 * d + 4],
                                     ps[:, 6, (q * 2 + d) * 24:(q * 2 + d + 1) * 24].rearrange("p (c x) -> p c x", x=4), ACT.Exp)
                a.activation(dex[:, 2, :, :], ps[:, 6, 96:144].rearrange("p (c x) -> p c x", x=8), ACT.Exp).then_inc(s["dex_ready"], 1)
            a.wait_ge(s["taps_done"], p + 1)
            a.activation(cq[:, :, :], cq[:, :, :], ACT.Silu)
            a.activation(ckv[:, :, :], ckv[:, :, :], ACT.Silu).then_inc(s["conv_done"], 1)
            a.wait_ge(s["tok_ps"], p + 1)
            flat = arena[:, R1:R1 + 4096]
            for n in range(4):
                last = a.activation(flat[:, n * BANK:(n + 1) * BANK], ps[:, n, :], ACT.Copy)
            last.then_inc(s["tok_out"], 1)
            a.wait_ge(s["qk_mean"], p + 1)
            a.activation(dss, dss, ACT.Sqrt).then_inc(s["qk_root"], 1)
            a.wait_ge(s["chan_ps"], p + 1)
            flat = arena[:, R2:R2 + 4096]
            for n in range(5):
                last = a.activation(flat[:, n * BANK:(n + 1) * BANK], ps[:, n, :], ACT.Copy)
            last.then_inc(s["chan_ready"], 1)
            for c in range(NC):
                a.wait_ge(s["sys_ps"], NC * p + c + 1)
                if c:
                    a.wait_ge(s["sys_out"], NC * p + c)
                a.activation(dec.rearrange("p d h x -> p (d h x)"), ps[:, 2 * (c % 2), :], ACT.Exp).then_inc(s["dec_ready"], 1)
            for u in range(NC, NC * LEVELS):
                w = NC * (LEVELS - 1) * p + u - NC
                a.wait_ge(s["M_ps"], w + 1)
                if u >= NC + 2:
                    a.wait_ge(s["inv_ps"], NC * LEVELS * p + u - 1)
                a.activation(Mb[u % 2].rearrange("p a x -> p (a x)"), ps[:, u % 2, :], ACT.Copy).then_inc(s["M_ready"], 1)

        def pool_dn(g, ch, p):
            hs = 2 * p
            g.wait_ge(s["chan_ready"], p + 1)
            g.wait_ge(s["lga_ready"], 1)
            for c in range(NC):
                if c:
                    g.wait_ge(s["sys_ps"], NC * p + c)
                for d in range(2):
                    last = g.tensor_tensor(mr[:, d, :, :], bc(cmask[:, d, :], [P, 2, P], 1),
                                           bc(lga[:, c, 4 * d + hs:4 * d + hs + 2], [P, 2, P], 2), ALU.mult)
                last.then_inc(s["mr_ready"], 1)
                if c >= 1:
                    mask_beta(g, ch, p, c - 1)
            mask_beta(g, ch, p, NC - 1)
            U0 = NC * LEVELS * p
            g.wait_ge(s["masked"], NC * (p + 1))
            for u in range(NC * LEVELS):
                l, c = divmod(u, NC)
                if NC + 2 > u >= 2:
                    g.wait_ge(s["inv_ps"], U0 + u - 1)
                    g.wait_ge(s["inv_out"], U0 + u - 1)
                elif u >= 2:
                    g.wait_ge(s["M_ps"], NC * (LEVELS - 1) * p + u - NC - 1)
                for d in range(2):
                    last = g.tensor_tensor(al[u % 2][:, 2 * d:2 * d + 2, :], AT[:, c, 2 * d:2 * d + 2, :],
                                           bc(levm[:, l, d, :], [P, 2, P], 1), ALU.mult)
                last.then_inc(s["al_ready"], 1)
            g.wait_ge(s["inv_out"], U0 + NC * LEVELS)
            for k in range(NC - 1):
                if k >= 2:
                    g.wait_ge(s["add_ps"], (NC - 1) * p + k - 1)
                for d in range(2):
                    c = ORDER[d][k]
                    last = g.tensor_tensor(kx[k % 2][:, 2 * d:2 * d + 2, :], tk[:, c, :, :],
                                           bc(dex[:, 1, c, 4 * d + hs:4 * d + hs + 2], [P, 2, P], 2), ALU.mult)
                last.then_inc(s["kx_ready"], 1)

        def mask_beta(g, ch, p, c):
            hs = 2 * p
            g.wait_ge(s["sys_out"], NC * p + c + 1)
            for d in range(2):
                v = AT[:, c, 2 * d:2 * d + 2, :]
                last = g.tensor_tensor(v, v, bc(bet[:, c, 4 * d + hs:4 * d + hs + 2], [P, 2, P], 2), ALU.mult)
                if c >= NCC:
                    w = dA[:, c - NCC, 2 * d:2 * d + 2, :]
                    last = g.tensor_tensor(w, w, bc(cmask[:, d, :], [P, 2, P], 1), ALU.mult)
            last.then_inc(s["masked"], 1)

        def dve_dn(v, ch, p):
            hs = 2 * p
            if p == 0:
                v.wait_ge(s["bet_ready"], 1)
                ba = ps[:, 7, 0:96].rearrange("p (c x) -> p c x", x=16)
                v.tensor_tensor(dtmp[:, 0], ba[:, :, 8:16], bc(aldt[:, 1, :], [P, NC, 8], 1), ALU.add).then_inc(s["dt_added"], 1)
                v.wait_ge(s["soft_ready"], 1)
                ch.link(v.tensor_scalar(dtmp[:, 2], dtmp[:, 0], 0.0, None, ALU.max))
                ch.link(v.tensor_tensor(dtmp[:, 1], dtmp[:, 1], dtmp[:, 2], ALU.add))
                ch.link(v.tensor_scalar(dtmp[:, 1], dtmp[:, 1], -1.0, None, ALU.mult))
                v.tensor_tensor(lga[:, :, :], dtmp[:, 1], bc(aldt[:, 0, :], [P, NC, 8], 1), ALU.mult).then_inc(s["lga_ready"], 1)
                v.wait_ge(s["dex_ready"], 1)
                v.tensor_scalar(nex[:, :, :], dex[:, 0, :, :], -1.0, None, ALU.mult)
            v.wait_ge(s["dnp_out"], DU * (p + 1))
            tiles = [(pq[:, h, :], cq[:, h, :], h + hs) for h in range(2)]
            tiles += [(pkv[:, j, CTX:], ckv[:, j, CTX:], 4 + 4 * (j // 2) + j % 2 + hs) for j in range(4)]
            ctiles = [(pkv[:, j, 0:CTX], ckv[:, j, 0:CTX], 4 + 4 * (j // 2) + j % 2 + hs) for j in range(4)]
            taps = [(0, 0)] + [(y, x) for y in (-1, 0, 1) for x in (-1, 0, 1) if (y, x) != (0, 0)]
            for y, x in taps:
                for src, dst, t in tiles:
                    w = col(2, ((y + 1) * 3 + x + 1) * 12 + t)
                    i = src.rearrange("p (r c) -> p r c", c=GRID_W)
                    o = dst.rearrange("p (r c) -> p r c", c=GRID_W)
                    r0, r1, c0, c1 = max(0, -y), GRID_R - max(0, y), max(0, -x), GRID_W - max(0, x)
                    o, i = o[:, r0:r1, c0:c1], i[:, r0 + y:r1 + y, c0 + x:c1 + x]
                    if (y, x) == (0, 0):
                        ch.mark(v.tensor_scalar(o, i, w, None, ALU.mult))
                    else:
                        ch.mark(v.scalar_tensor_tensor(out=o, in0=i, scalar=w, in1=o, op0=ALU.mult, op1=ALU.add))
                if y == 0:
                    for src, dst, t in ctiles:
                        w = col(2, (3 + x + 1) * 12 + t)
                        c0, c1 = max(0, -x), CTX - max(0, x)
                        o, i = dst[:, c0:c1], src[:, c0 + x:c1 + x]
                        if x == 0:
                            ch.mark(v.tensor_scalar(o, i, w, None, ALU.mult))
                        else:
                            ch.mark(v.scalar_tensor_tensor(out=o, in0=i, scalar=w, in1=o, op0=ALU.mult, op1=ALU.add))
                ch.wait()
            v.sem_inc(s["taps_done"], 1)
            v.wait_ge(s["tok_ps"], p + 1)
            flat = arena[:, R1:R1 + 4096]
            for n in range(4, 8):
                last = v.tensor_copy(flat[:, n * BANK:(n + 1) * BANK], ps[:, n, :])
            ch.link(last)
            v.sem_inc(s["tok_out"], 1)
            v.wait_ge(s["tok_out"], 2 * (p + 1))
            qk = arena[:, R1:R1 + 2560].rearrange("p (a x) -> p a x", x=P)
            sqv = sq.rearrange("p a b c -> p (a b) c")[:, 0:20, :]
            ch.link(v.tensor_tensor(sqv, qk, qk, ALU.mult))
            ch.link(v.reduce_sum(dss, sqv, axis=X))
            v.tensor_scalar(dss, dss, EPS, None, ALU.add).then_inc(s["qk_mean"], 1)
            v.wait_ge(s["qk_root"], p + 1)
            ch.link(v.reciprocal(dss, dss))
            ch.link(v.tensor_scalar(dss[:, 0:8], dss[:, 0:8], float(P) ** -0.5, None, ALU.mult))
            v.tensor_tensor(qk, qk, bc(dss, [P, 20, P], 2), ALU.mult).then_inc(s["qk_normed"], 1)
            for c in range(NC):
                v.wait_ge(s["dec_ready"], NC * p + c + 1)
                kq = ps[:, 2 * (c % 2) + 1, :].rearrange("p (a h x) -> p a h x", a=2, h=2)
                for d in range(2):
                    last = v.tensor_tensor(AT[:, c, 2 * d:2 * d + 2, :], kq[:, 0], dec[:, d], ALU.mult)
                    if c >= NCC:
                        last = v.tensor_tensor(dA[:, c - NCC, 2 * d:2 * d + 2, :], kq[:, 1], dec[:, d], ALU.mult)
                last.then_inc(s["sys_out"], 1)
            U0 = NC * LEVELS * p
            idb = bc(ident[:, :], [P, 4, P], 1)
            for u in range(NC * LEVELS):
                l, c = divmod(u, NC)
                v.wait_ge(s["inv_ps"], U0 + u + 1)
                if l == 0:
                    v.tensor_tensor(XT[:, c], idb, al[c % 2], ALU.subtract)
                    last = v.tensor_tensor(XI[:, c], idb, ps[:, 4 + u % 2, :].rearrange("p (a x) -> p a x", a=4), ALU.subtract)
                else:
                    v.wait_ge(s["inv_out"], U0 + u - NC + 1)
                    if l < LEVELS - 1:
                        v.tensor_tensor(XI[:, c], XI[:, c], ps[:, 2 + u % 2, :].rearrange("p (a x) -> p a x", a=4), ALU.subtract)
                    last = v.tensor_tensor(XT[:, c], XT[:, c], ps[:, 4 + u % 2, :].rearrange("p (a x) -> p a x", a=4), ALU.subtract)
                last.then_inc(s["inv_out"], 1)
            for k in range(NC):
                if k:
                    v.wait_ge(s["ks_ps"], (NC - 1) * p + k)
                    for d in range(2):
                        c = ORDER[d][k]
                        for h in range(2):
                            a = 2 * d + h
                            last = v.scalar_tensor_tensor(out=zb[:, a, :], in0=ps[:, 0, a * P:(a + 1) * P],
                                                          scalar=nex[:, c, 4 * d + hs + h:4 * d + hs + h + 1],
                                                          in1=tv[:, c, h, :], op0=ALU.mult, op1=ALU.add)
                    last.then_inc(s["z_ready"], 1)
                v.wait_ge(s["u_ps"], NC * p + k + 1)
                for d in range(2):
                    c = ORDER[d][k]
                    last = v.tensor_tensor(dU[:, c, 2 * d:2 * d + 2, :], ps[:, 1, 2 * d * P:2 * (d + 1) * P].rearrange("p (h x) -> p h x", h=2),
                                           bc(bet[:, c, 4 * d + hs:4 * d + hs + 2], [P, 2, P], 2), ALU.mult)
                last.then_inc(s["u_ready"], 1)
                if k < NC - 1:
                    v.wait_ge(s["add_ps"], (NC - 1) * p + k + 1)
                    if k == 0:
                        last = v.tensor_copy(dS[:, 0].rearrange("p a x -> p (a x)"), ps[:, 2, :])
                    else:
                        for d in range(2):
                            c = ORDER[d][k]
                            for h in range(2):
                                a = 2 * d + h
                                last = v.scalar_tensor_tensor(out=dS[:, k, a, :], in0=dS[:, k - 1, a, :],
                                                              scalar=dex[:, 2, c, 4 * d + hs + h:4 * d + hs + h + 1],
                                                              in1=ps[:, 2, a * P:(a + 1) * P], op0=ALU.mult, op1=ALU.add)
                    last.then_inc(s["dS_ready"], 1)
                    v.wait_ge(s["dS_ready"], (NC - 1) * p + k + 1)
            for c in range(NX):
                b = 3 + 2 * (c % 2)
                v.wait_ge(s["do_ps"], NX * p + c + 1)
                if c:
                    v.wait_ge(s["do_out"], NX * p + c)
                for d in range(2):
                    ch.mark(v.tensor_tensor(zb[:, 2 * d:2 * d + 2, :], ps[:, b, 2 * d * P:2 * (d + 1) * P].rearrange("p (h x) -> p h x", h=2),
                                            bc(dex[:, 0, NCC + c, 4 * d + hs:4 * d + hs + 2], [P, 2, P], 2), ALU.mult))
                ch.wait()
                ch.link(v.tensor_tensor(zb[:, 0:2, :], zb[:, 0:2, :], zb[:, 2:4, :], ALU.add))
                v.tensor_tensor(o_sb[:, c, 512 + p * CW:512 + (p + 1) * CW].rearrange("p (h x) -> p h x", h=2),
                                zb[:, 0:2, :], ps[:, b + 1, 0:2 * P].rearrange("p (h x) -> p h x", h=2), ALU.add).then_inc(s["do_out"], 1)


        class Tally(dict):
            def __missing__(self, name):
                return 0

        tally = {e: Tally() for e in ("sp", "pe", "act", "dve", "pool")}

        def pe_transpose_in(pe, src, T):
            n = tally["pe"]["srcT"] = tally["pe"]["srcT"] + 1
            pe.wait_ge(s["srcT_ready"], n)
            for k in range(KD):
                for m in range(T):
                    last = pe.transpose(ps[:, k, m * P:(m + 1) * P], src[:, m, k * P:(k + 1) * P], ident[:, :])
                last.then_inc(s["srcT_ps"], 1)

        def act_transpose_out(a):
            n = tally["act"]["srcT"]
            for k in range(1, KD, 2):
                a.wait_ge(s["srcT_ps"], KD * n + k + 1)
                last = a.activation(hT[:, k, :], ps[:, k, :], ACT.Copy)
            last.then_inc(s["hT_act"], 1)
            tally["act"]["srcT"] = n + 1

        def dve_transpose_out(v):
            n = tally["dve"]["srcT"]
            for k in range(0, KD, 2):
                v.wait_ge(s["srcT_ps"], KD * n + k + 1)
                last = v.tensor_copy(hT[:, k, :], ps[:, k, :])
            last.then_inc(s["hT_dve"], 1)
            tally["dve"]["srcT"] = n + 1

        TP = 4

        def pe_out(pe, W):
            n = tally["pe"]["out"]
            pe.wait_ge(s["hT_act"], n + 1)
            pe.wait_ge(s["hT_dve"], n + 1)
            for q in range(4):
                w = W.take(KD)
                for m in range(NX):
                    u = 4 * q + m
                    if u >= 8:
                        pe.wait_ge(s["gated"], 16 * n + u - 7)
                    for k in range(KD):
                        last = pe.matmul(ps[:, u % 8, 0:CW], hT[:, k, m * P:(m + 1) * P], w[:, k, :],
                                         start=(k == 0), stop=(k == KD - 1))
                        if k == 0:
                            W.pay(last)
                    last.then_inc(s["out_ps"], 1)
                W.done()
            W.pay()
            tally["pe"]["out"] = n + 1

        def dve_out(v, tmp):
            n = tally["dve"]["out"]
            for u in range(16):
                q, m = divmod(u, 4)
                v.wait_ge(s["out_ps"], 16 * n + u + 1)
                if u >= TP:
                    v.wait_ge(s["added"], 16 * n + u - TP + 1)
                v.tensor_tensor(tmp[:, u % TP, :], ps[:, u % 8, 0:CW], gate[:, 0, q * CW:(q + 1) * CW],
                                ALU.mult).then_inc(s["gated"], 1)
            tally["dve"]["out"] = n + 1

        def pool_out(g, tmp):
            n = tally["pool"]["out"]
            for u in range(16):
                q, m = divmod(u, 4)
                g.wait_ge(s["gated"], 16 * n + u + 1)
                x = xres[:, m, q * CW:(q + 1) * CW]
                g.tensor_tensor(x, x, tmp[:, u % TP, :], ALU.add).then_inc(s["added"], 1)
            tally["pool"]["out"] = n + 1

        def sp_out(W, w):
            v = w.rearrange("(k p) n -> p k n", p=P)
            for q in range(4):
                W.load(cols_of(v, q * CW))

        wo_sq = at(4096, NX, 8, P)
        wo_tmp = at(8192, TP, CW)
        hss = stat[:, 0:32]

        def act_wout(a):
            a.wait_ge(s["head_mean"], 1)
            a.activation(hss, hss, ACT.Sqrt).then_inc(s["head_root"], 1)
            a.wait_ge(s["srcT_ready"], 1)
            for m in range(NX):
                a.dma_start(xres[:, m, :], ins["x"][0, m * P:(m + 1) * P, :]).then_inc(s["x_back"], 16)
            act_transpose_out(a)

        def dve_wout(v, ch):
            o3 = o_sb[:, :, :].rearrange("p m (h x) -> p (m h) x", x=P)
            ch.link(v.tensor_tensor(wo_sq.rearrange("p m h x -> p (m h) x"), o3, o3, ALU.mult))
            ch.link(v.reduce_sum(hss, wo_sq.rearrange("p m h x -> p (m h) x"), axis=X))
            v.tensor_scalar(hss, hss, 1.0 / P, EPS, ALU.mult, ALU.add).then_inc(s["head_mean"], 1)
            v.wait_ge(s["head_root"], 1)
            ch.link(v.reciprocal(hss, hss))
            ch.link(v.tensor_tensor(o3, o3, bc(hss, [P, 32, P], 2), ALU.mult))
            ch.link(v.tensor_tensor(o3, o3, gz[:, :, :].rearrange("p m (h x) -> p (m h) x", x=P), ALU.mult))
            for b in range(2):
                for m in range(NX):
                    o = o_sb[:, m, b * 512:(b + 1) * 512].rearrange("p (h x) -> p h x", x=P)
                    last = v.tensor_tensor(o, o, bc(hgw[:, b, :], [P, 4, P], 1), ALU.mult)
            last.then_inc(s["srcT_ready"], 1)
            dve_transpose_out(v)
            dve_out(v, wo_tmp)

        def pe_wout(pe, W):
            pe_transpose_in(pe, o_sb, NX)
            pe_out(pe, W)

        def pool_wout(g):
            g.wait_ge(s["x_back"], 64)
            pool_out(g, wo_tmp)

        wr = at(4096, KD, 20)
        br = at(4096 + 160, 20)
        lg = at(4300, NX, 20)
        rt = at(4500, 12, NX, 4)
        re4 = at(4700, NX, 4, 4)
        N_PAIR = 2 * SEQ
        ITEMS = N_PAIR // P + N_EXP - 1
        mo = Place(5120)
        aT = mo(4, P)
        sg = mo(4, P)
        yacc = mo(NX, D)
        xg = mo(KD, P)
        pick = mo(NX, P)
        put = mo(SEQ)
        puts = mo(2, SEQ)
        ysb = mo(D)
        rows_of = mo(2, 2, SEQ)
        diag = mo(2, 2, NX, P)
        iota = mo(P)
        slot0 = mo(1)
        sel = mo(2, NX, N_EXP)
        both = mo(NX, N_EXP)
        rank = mo(NX, N_EXP)
        tmp_e = mo(2, NX, N_EXP)
        slot = mo(2, NX)
        wgt = mo(2, NX)
        n_e = mo(N_EXP)
        c_e = mo(3, N_EXP)
        item_e = mo(ITEMS, N_EXP)
        item_f = mo(ITEMS)
        assert mo.off <= ARENA

        def sp_router(sp):
            sp.wait_ge(s["stage_done"], 4 * (STAGES.index("wout") + 1 - len(skip)))
            sp.dma_start(wr[:, :, 0:4], ins["w_group"][0].rearrange("(k p) n -> p k n", p=P)).then_inc(s["router_in"], 16)
            sp.dma_start(wr[:, :, 4:20], ins["w_expert"][0].rearrange("(k p) n -> p k n", p=P)).then_inc(s["router_in"], 16)
            sp.dma_start(br[0:1, 0:4], ins["b_group"]).then_inc(s["router_in"], 16)
            sp.dma_start(br[0:1, 4:20], ins["b_expert"]).then_inc(s["router_in"], 16)

        def sp_moe(sp, W):
            sp.wait_ge(s["item_experts"], 1)
            with sp.Fori(0, ITEMS) as i:
                W.loop(i, RING)
                e = sp.value_load(etab[0:1, bass.ds(i, 1)], min_val=0, max_val=N_EXP - 1)
                up = [ins[n][0][bass.ds(e, 1), :, :].rearrange("a (k p) n -> p (a k) n", p=P) for n in ("w_gate", "w_up")]
                dn = ins["w_down"][0][bass.ds(e, 1), :, :].rearrange("a (k p) n -> p (a k) n", p=P)
                for half in range(2):
                    for w in up:
                        W.load(cols_of(w, half * CW))
                for half in range(2):
                    W.load(dn[:, :, half * 512:(half + 1) * 512])
            W.end(ITEMS)

        def pe_moe(pe, W):
            pe_norm(pe, NX, xn_buf)
            pe.wait_ge(s["router_in"], 64)
            pe.wait_ge(s["h2_act"], 1)
            pe.wait_ge(s["h2_dve"], 1)
            for m in range(NX):
                o = ps[:, 0, m * 20:(m + 1) * 20]
                for k in range(KD):
                    pe.matmul(o, hT[:, k, m * P:(m + 1) * P], wr[:, k, :], start=(k == 0), stop=False)
                last = pe.matmul(o, ones[0:1, :], br[0:1, :], start=False, stop=True)
            pe.matmul(ps[:, 1, 128:256], ones[:, :], cmask[:, 3, :], start=True, stop=True)
            last = pe.matmul(ps[:, 1, 256:257], cmask[:, 3, :], ones[:, 0:1], start=True, stop=True)
            last.then_inc(s["router_ps"], 1)
            pe.wait_ge(s["router_dve"], 1)
            for m in range(NX):
                o = ps[:, 2, m * N_EXP:(m + 1) * N_EXP]
                for b in range(m):
                    pe.matmul(o, ones[:, :], both[:, b, :], start=(b == 0), stop=False)
                pe.matmul(o, cmask[:, 3, :], both[:, m, :], start=(m == 0), stop=True)
            for m in range(NX):
                last = pe.matmul(ps[:, 2, NX * N_EXP:(NX + 1) * N_EXP], ones[:, :], both[:, m, :],
                                 start=(m == 0), stop=(m == NX - 1))
            last.then_inc(s["router_ps"], 1)
            pe.wait_ge(s["router_dve"], 2)
            for q in range(4):
                for m in range(NX):
                    last = pe.matmul(ps[:, 4 + q, m * P:(m + 1) * P], ones[:, :], diag[:, q // 2, q % 2, m, :],
                                     start=True, stop=True)
            last.then_inc(s["router_ps"], 1)

            def gather():
                for b in range(2):
                    for k in range(4 * b, 4 * b + 4):
                        for m in range(NX):
                            last = pe.matmul(ps[:, 4 + b, (k % 4) * P:(k % 4 + 1) * P],
                                             xn_buf[:, m, k * P:(k + 1) * P], pick[:, m, :],
                                             start=(m == 0), stop=(m == NX - 1))
                            W.pay(last)
                    last.then_inc(s["moe_ps"], 1)

            pe.wait_ge(s["moe_dve"], 1)
            gather()
            with pe.Fori(0, ITEMS) as i:
                W.loop(i, RING)
                pe.wait_ge(s["moe_act"], i * 5 + 3)
                for f in range(4):
                    w = W.take(KD)
                    pe.wait_ge(s["moe_dve"], i * 13 + 6 + f)
                    for j in range(2):
                        for k in range(KD):
                            last = pe.matmul(ps[:, f, j * P:(j + 1) * P], w[:, k, j * P:(j + 1) * P], xg[:, k, :],
                                             start=(k == 0), stop=(k == KD - 1))
                            if j == 0 and k == 0:
                                W.pay(last)
                    last.then_inc(s["moe_ps"], 1)
                    W.done()
                pe.wait_ge(s["moe_dve"], i * 13 + 15)
                gather()
                for half in range(2):
                    w = W.take(4)
                    for k in range(4):
                        if half == 0 and k % 2 == 0:
                            pe.wait_ge(s["moe_dve"], i * 13 + 16 + k // 2)
                        last = pe.matmul(ps[:, 6 + half, :], aT[:, k, :], w[:, k, :], start=(k == 0), stop=(k == 3))
                        if k == 0:
                            W.pay(last)
                    last.then_inc(s["moe_ps"], 1)
                    W.done()
                pe.wait_ge(s["moe_dve"], i * 13 + 18)
                for half in range(2):
                    pe.wait_ge(s["moe_act"], i * 5 + 9 + half)
                    for m in range(NX):
                        last = pe.matmul(ps[:, 4 * half + m, :], put[:, m * P:(m + 1) * P],
                                         ysb[:, half * 512:(half + 1) * 512], start=True, stop=True)
                        last.then_inc(s["moe_ps"], 1)
                W.pay()
            W.end(ITEMS)

        def act_moe(a):
            act_norm(a, xres, NX, njunk, hT, 1, 0, xn_buf, stat[:, 0:4], 2 * KD)
            a.drain().then_inc(s["h2_act"], 1)
            a.wait_ge(s["router_exp"], 1)
            a.activation(rt[:, 3], rt[:, 3], ACT.Exp).then_inc(s["router_act"], 1)
            a.wait_ge(s["router_exp"], 2)
            a.activation(rt[:, 9, :, 0:1], rt[:, 9, :, 0:1], ACT.Exp).then_inc(s["router_act"], 1)

            def gathered(ps_count, inc):
                a.wait_ge(s["moe_ps"], ps_count)
                for k in range(4, KD):
                    last = a.activation(xg[:, k, :], ps[:, 5, (k - 4) * P:(k - 3) * P], ACT.Identity,
                                        bias=modc[:, 2 * KD + k, 0:1], scale=mcol[:, 1, 0, k:k + 1])
                last.then_inc(s["moe_act"], inc)

            gathered(2, 5)
            with a.Fori(0, ITEMS) as i:
                for h in range(2):
                    a.wait_ge(s["moe_ps"], i * 16 + 3 + 2 * h)
                    a.wait_ge(s["moe_dve"], i * 13 + 3 + h)
                    a.activation(sg[:, 2 * h:2 * h + 2, :], ps[:, 2 * h, 0:256].rearrange("p (j t) -> p j t", j=2),
                                 ACT.Silu).then_inc(s["moe_act"], 1)
                gathered(i * 16 + 8, 1)
                for h in range(2):
                    a.wait_ge(s["moe_ps"], i * 16 + 9 + h)
                    a.copy(ysb[:, h * 512:(h + 1) * 512], ps[:, 6 + h, :]).then_inc(s["moe_act"], 1)

        def first_of(v, ch, dst, eq, pre):
            ch.mark(v.memset(pre[:, :, 0:1], 0.0))
            ch.link(v.tensor_copy(pre[:, :, 1:2], eq[:, :, 0:1]))
            ch.link(v.tensor_tensor(pre[:, :, 2:3], pre[:, :, 1:2], eq[:, :, 1:2], ALU.add))
            ch.link(v.tensor_tensor(pre[:, :, 3:4], pre[:, :, 2:3], eq[:, :, 2:3], ALU.add))
            ch.link(v.tensor_scalar(pre, pre, 0.0, None, ALU.is_equal))
            ch.link(v.tensor_tensor(dst, eq, pre, ALU.mult))

        def dve_router(v, ch):
            G, E = lg[:, :, 0:4], lg[:, :, 4:20].rearrange("p m (g e) -> p m g e", g=4)
            mx, eq, og, dg, gw, ei, o1, o2, e2, mm, w4, pre = (rt[:, j] for j in range(12))
            v.wait_ge(s["router_ps"], 1)
            ch.link(v.tensor_copy(lg[:, :, :], ps[:, 0, 0:80].rearrange("p (m n) -> p m n", n=20)))
            b4 = [P, NX, 4]
            ch.link(v.reduce_max(mx[:, :, 0:1], G, axis=X))
            ch.link(v.tensor_tensor(eq, G, mx[:, :, 0:1].broadcast_to(b4), ALU.is_equal))
            v.tensor_tensor(dg, G, mx[:, :, 0:1].broadcast_to(b4), ALU.subtract).then_inc(s["router_exp"], 1)
            first_of(v, ch, og, eq, pre)
            v.wait_ge(s["router_act"], 1)
            ch.link(v.reduce_sum(gw[:, :, 0:1], dg, axis=X))
            ch.link(v.reciprocal(gw[:, :, 0:1], gw[:, :, 0:1]))
            ch.link(v.tensor_tensor(re4, E, bc(og, [P, NX, 4, 4], 3), ALU.mult))
            ch.link(v.reduce_sum(ei, re4.rearrange("p m g e -> p m e g"), axis=X))
            ch.link(v.reduce_max(mx[:, :, 1:2], ei, axis=X))
            ch.link(v.tensor_tensor(eq, ei, mx[:, :, 1:2].broadcast_to(b4), ALU.is_equal))
            first_of(v, ch, o1, eq, pre)
            ch.link(v.scalar_tensor_tensor(out=e2, in0=o1, scalar=-1e30, in1=ei, op0=ALU.mult, op1=ALU.add))
            ch.link(v.reduce_max(mx[:, :, 2:3], e2, axis=X))
            ch.link(v.tensor_tensor(eq, e2, mx[:, :, 2:3].broadcast_to(b4), ALU.is_equal))
            first_of(v, ch, o2, eq, pre)
            v.tensor_tensor(mm[:, :, 0:1], mx[:, :, 2:3], mx[:, :, 1:2], ALU.subtract).then_inc(s["router_exp"], 1)
            v.wait_ge(s["router_act"], 2)
            ch.link(v.tensor_scalar(mm[:, :, 1:2], mm[:, :, 0:1], 1.0, None, ALU.add))
            ch.link(v.reciprocal(mm[:, :, 1:2], mm[:, :, 1:2]))
            ch.link(v.tensor_tensor(mm[:, :, 1:2], mm[:, :, 1:2], gw[:, :, 0:1], ALU.mult))
            ch.link(v.tensor_tensor(mm[:, :, 2:3], mm[:, :, 0:1], mm[:, :, 1:2], ALU.mult))
            for j, o in enumerate((o1, o2)):
                ch.mark(v.tensor_copy(wgt[:, j, :], mm[:, :, 1 + j]))
                ch.mark(v.tensor_tensor(sel[:, j].rearrange("p m (g e) -> p m g e", g=4), bc(og, [P, NX, 4, 4], 3),
                                        bc(o, [P, NX, 4, 4], 2), ALU.mult))
            ch.wait()
            v.tensor_tensor(both, sel[:, 0], sel[:, 1], ALU.add).then_inc(s["router_dve"], 1)
            ch.mark(v.tensor_copy(iota, ps[:, 1, 128:256]))
            ch.mark(v.tensor_copy(slot0, ps[:, 1, 256:257]))
            v.wait_ge(s["router_ps"], 2)
            ch.mark(v.tensor_copy(rank, ps[:, 2, 0:NX * N_EXP].rearrange("p (m e) -> p m e", m=NX)))
            ch.link(v.tensor_copy(n_e, ps[:, 2, NX * N_EXP:(NX + 1) * N_EXP]))
            ch.link(v.tensor_scalar(c_e[:, 0, :], n_e, 0.0, None, ALU.is_gt))
            for k in range(1, SEQ // P):
                ch.link(v.scalar_tensor_tensor(out=c_e[:, 0, :], in0=n_e, scalar=thr[:, k:k + 1], in1=c_e[:, 0, :],
                                               op0=ALU.is_gt, op1=ALU.add))
            ch.link(v.tensor_copy(c_e[:, 1, :], c_e[:, 0, :]))
            cur, d = 1, 1
            while d < N_EXP:
                nxt = 3 - cur
                ch.mark(v.tensor_copy(c_e[:, nxt, 0:d], c_e[:, cur, 0:d]))
                ch.link(v.tensor_tensor(c_e[:, nxt, d:], c_e[:, cur, d:], c_e[:, cur, 0:N_EXP - d], ALU.add))
                cur, d = nxt, 2 * d
            ch.link(v.tensor_tensor(item_e, bc(c_e[:, cur, :], [P, ITEMS, N_EXP], 1),
                                    bc(iota[:, 0:ITEMS], [P, ITEMS, N_EXP], 2), ALU.is_le))
            ch.link(v.reduce_sum(item_f, item_e, axis=X))
            ch.link(v.tensor_scalar(item_f, item_f, float(N_EXP - 1), None, ALU.min))
            v.tensor_copy(etab[:, 0:ITEMS], item_f).then_inc(s["item_experts"], 1)
            ch.link(v.tensor_tensor(c_e[:, 0, :], c_e[:, cur, :], c_e[:, 0, :], ALU.subtract))
            ch.link(v.scalar_tensor_tensor(out=rank, in0=bc(c_e[:, 0, :], [P, NX, N_EXP], 1), scalar=thr[:, 1:2],
                                           in1=rank, op0=ALU.mult, op1=ALU.add))
            for j in range(2):
                ch.mark(v.tensor_tensor(tmp_e[:, j], sel[:, j], rank, ALU.mult))
            ch.wait()
            for j in range(2):
                ch.mark(v.reduce_sum(slot[:, j, :], tmp_e[:, j], axis=X))
            ch.wait()
            for j in range(2):
                for m in range(NX):
                    v.tensor_scalar(diag[:, 0, j, m, :], ident[:, :], slot[:, j, m:m + 1], None, ALU.mult)
                    last = v.tensor_scalar(diag[:, 1, j, m, :], ident[:, :], wgt[:, j, m:m + 1], None, ALU.mult)
            last.then_inc(s["router_dve"], 1)
            v.wait_ge(s["router_ps"], 3)
            for q in range(4):
                ch.mark(v.tensor_copy(rows_of[:, q // 2, q % 2, :], ps[:, 4 + q, :]))
            ch.wait()

        def dve_moe(v, ch):
            dve_norm(v, ch, xres, NX, hT, 1, 0, xn_buf, stat[:, 0:4], 2 * KD)
            v.drain().then_inc(s["h2_dve"], 1)
            dve_router(v, ch)
            ch.link(v.memset(yacc[:, :, :], 0.0))

            def build_pick():
                for m in range(NX):
                    ch.mark(v.tensor_scalar(pick[:, m, :], iota, slot[:, 0, m:m + 1], None, ALU.is_equal))
                ch.wait()
                for m in range(NX):
                    last = v.scalar_tensor_tensor(out=pick[:, m, :], in0=iota, scalar=slot[:, 1, m:m + 1],
                                                  in1=pick[:, m, :], op0=ALU.is_equal, op1=ALU.add)
                last.then_inc(s["moe_dve"], 1)

            def gathered(ps_count, inc):
                v.wait_ge(s["moe_ps"], ps_count)
                for k in range(4):
                    last = v.tensor_scalar(xg[:, k, :], ps[:, 4, k * P:(k + 1) * P], mcol[:, 1, 0, k:k + 1],
                                           modc[:, 2 * KD + k, 0:1], ALU.mult, ALU.add)
                last.then_inc(s["moe_dve"], inc)

            build_pick()
            gathered(1, 12)
            with v.Fori(0, ITEMS) as i:
                ch.loop(i, 8)
                v.wait_ge(s["moe_ps"], i * 16 + 2)
                v.wait_ge(s["moe_dve"], i * 13 + 13)
                for j in range(2):
                    ch.mark(v.scalar_tensor_tensor(out=puts[:, j, :], in0=rows_of[:, 0, j, :], scalar=slot0,
                                                   in1=rows_of[:, 1, j, :], op0=ALU.is_equal, op1=ALU.mult))
                ch.mark(v.tensor_scalar(slot[:, :, :], slot[:, :, :], float(-P), None, ALU.add))
                ch.wait()
                v.tensor_tensor(put, puts[:, 0, :], puts[:, 1, :], ALU.add).then_inc(s["moe_dve"], 1)
                ch.mark(v.tensor_scalar(slot0, slot0, float(P), None, ALU.add))
                build_pick()
                for h in range(2):
                    v.wait_ge(s["moe_ps"], i * 16 + 4 + 2 * h)
                    v.wait_ge(s["moe_act"], i * 5 + 6 + h)
                    v.tensor_tensor(aT[:, 2 * h:2 * h + 2, :], sg[:, 2 * h:2 * h + 2, :],
                                    ps[:, 2 * h + 1, 0:256].rearrange("p (j t) -> p j t", j=2),
                                    ALU.mult).then_inc(s["moe_dve"], 1)
                gathered(i * 16 + 7, 1)
                for n in range(8):
                    half, m = divmod(n, 4)
                    v.wait_ge(s["moe_ps"], i * 16 + 11 + n)
                    y = yacc[:, m, half * 512:(half + 1) * 512]
                    v.tensor_tensor(y, y, ps[:, n, :], ALU.add).then_inc(s["moe_dve"], 1)
            ch.end(ITEMS)
            v.wait_ge(s["moe_dve"], 13 * (ITEMS + 1))
            for m in range(NX):
                ch.mark(v.tensor_tensor(yacc[:, m, :], yacc[:, m, :], gate[:, 1, :], ALU.mult))
            ch.wait()
            for m in range(NX):
                last = v.tensor_tensor(xres[:, m, :], xres[:, m, :], yacc[:, m, :], ALU.add)
            last.then_inc(s["x_done"], 1)

        def act_final(a, i, w):
            a.wait_ge(s["x_done"], (MOE if i else 0) + 1)
            a.dma_start(gate[:, 0, :], w.rearrange("(a n) -> a n", a=1).broadcast_to([P, D])).then_inc(s["fw_in"], 16)
            act_norm(a, xres, NX, njunk, None, 0, 0, xn_buf, stat[:, 0:4], 0)

        def dve_final(v, ch, i):
            n = nidx["dve"] = nidx["dve"] + 1
            ss = stat[:, 0:4]
            v.wait_ge(s["sumsq"], n)
            v.tensor_scalar(ss, ss, 1.0 / D, EPS, ALU.mult, ALU.add).then_inc(s["mean_ready"], 1)
            v.wait_ge(s["root"], n)
            ch.link(v.reciprocal(ss, ss))
            v.wait_ge(s["fw_in"], 16 * ((MOE if i else 0) + 1))
            for m in range(NX):
                last = v.scalar_tensor_tensor(out=xres[:, m, :], in0=xres[:, m, :], scalar=ss[:, m:m + 1], in1=gate[:, 0, :],
                                              op0=ALU.mult, op1=ALU.mult)
                last.then_inc(s["final_ready"], 1)


        HD = 64
        NH = 26
        RW = NH * HD
        raw = at(0, NX, RW)
        roped = at(6656, NX, RW)
        ctk = at(13312, NCC, 640)
        V = at(14592, NC, 640)
        cs = at(18432, 2, NX, 32)
        rtmp = [at(18688 + 832 * j, NH, 32) for j in range(4)]
        aQT = hT[:, :, :]
        aKT = at(0, 5, TOK)
        qkw = at(22016, 2, HD)
        lamv = at(22144, 4, HD)
        lams = aldt[:, 0, 0:4]
        subw = hgw[:, 0, :]
        hsq = at(3840, NX, 10, HD)
        AW = ins["attn_w_in_2"][0].rearrange("(k p) n -> p k n", p=P)
        APIECES = [[(0, 256, "raw", 0)], [(0, 256, "raw", 256)], [(0, 256, "rk", 512)], [(0, 256, "rk", 768)],
                   [(0, 256, "v", 0)], [(0, 256, "v", 256)], [(0, 256, "qb", 0)], [(0, 256, "qb", 1)],
                   [(0, 128, "rk", 1536), (128, 256, "v", 512)]]
        AUNITS = [(q, m) for q in range(9) for m in (range(NC) if q not in (0, 1, 6, 7) else range(NCC, NC))]

        def sp_proj(sp, W):
            for q in range(9):
                W.load(cols_of(AW, q * CW))
            sp.wait_ge(s["stage_done"], 4 * (STAGES.index("norm2") + 1 - len(skip)))
            sp.dma_start(cs[:, :, :, :], ins["rope"].rearrange("a (m p) f -> p a m f", p=P)).then_inc(s["attn_in"], 16)
            sp.dma_start(qkw[:, 0, :], ins["gqa_q_norm_2"].broadcast_to([P, HD])).then_inc(s["attn_in"], 16)
            sp.dma_start(qkw[:, 1, :], ins["gqa_k_norm_2"].broadcast_to([P, HD])).then_inc(s["attn_in"], 16)
            for j, n in enumerate(("diff_lq1_2", "diff_lk1_2", "diff_lq2_2", "diff_lk2_2")):
                sp.dma_start(lamv[:, j, :], ins[n].broadcast_to([P, HD])).then_inc(s["attn_in"], 16)
            sp.dma_start(subw[:, :], ins["diff_subln_2"].broadcast_to([P, P])).then_inc(s["attn_in"], 16)

        def pe_aproj(pe, W):
            w, q0 = None, -1
            for u, (q, m) in enumerate(AUNITS):
                if q != q0:
                    if w is not None:
                        W.done()
                    w, q0 = W.take(KD), q
                if u >= 8:
                    pe.wait_ge(s["ap_act" if u % 2 == 0 else "ap_dve"], (u - 8) // 2 + 1)
                src, mm = (hcT, m) if m < NCC else (hT, m - NCC)
                for k in range(KD):
                    last = pe.matmul(ps[:, u % 8, 0:CW], src[:, k, mm * P:(mm + 1) * P], w[:, k, :],
                                     start=(k == 0), stop=(k == KD - 1))
                    if k == 0:
                        W.pay(last)
                last.then_inc(s["ap_ps"], 1)
            W.done()
            W.pay()

        def aproj_out(eng, mine, copy, sem):
            for u, (q, m) in enumerate(AUNITS):
                if u % 2 != mine:
                    continue
                eng.wait_ge(s["ap_ps"], u + 1)
                for c0, c1, kind, off in APIECES[q]:
                    n = c1 - c0
                    if kind == "qb":
                        dst = raw[:, m - NCC, 1024:1536].rearrange("p (h two x) -> p two h x", two=2, x=HD)[:, off]
                        last = copy(dst, ps[:, u % 8, 0:CW].rearrange("p (h x) -> p h x", x=HD))
                        continue
                    if kind == "v":
                        dst = V[:, m, off:off + n]
                    elif m < NCC:
                        dst = ctk[:, m, (off - 512 if off < 1024 else 512):][:, 0:n]
                    else:
                        dst = raw[:, m - NCC, off:off + n]
                    last = copy(dst, ps[:, u % 8, c0:c1])
                last.then_inc(s[sem], 1)

        qss = stat[:, 0:40].rearrange("p (m h) -> p m h", h=10)
        css = stat[:, 40:44].rearrange("p (m h) -> p m h", h=2)

        def act_rope(a, ch):
            a.wait_ge(s["lam_sums"], 1)
            a.activation(lams[:, 0:2], lams[:, 0:2], ACT.Exp).then_inc(s["lam_exp"], 1)
            a.wait_ge(s["qk2_mean"], 1)
            a.activation(stat[:, 0:44], stat[:, 0:44], ACT.Sqrt).then_inc(s["qk2_root"], 1)
            heads_out(a, 1, lambda o, i: a.activation(o, i, ACT.Copy), "heads_act")

        def dve_rope(v, ch):
            v.wait_ge(s["attn_in"], 16 * 8)
            l4 = lamv[:, :, :].rearrange("p (a b) x -> p a b x", b=2)
            ch.link(v.tensor_tensor(l4[:, :, 0, :], l4[:, :, 0, :], l4[:, :, 1, :], ALU.mult))
            v.reduce_sum(lams[:, 0:2], l4[:, :, 0, :], axis=X).then_inc(s["lam_sums"], 1)
            q = raw[:, :, 1024:1664].rearrange("p m (h x) -> p m h x", x=HD)
            c = ctk[:, :, 512:640].rearrange("p m (h x) -> p m h x", x=HD)
            qs = roped[:, :, 0:640].rearrange("p m (h x) -> p m h x", x=HD)
            cq2 = roped[:, 0:2, 640:768].rearrange("p m (h x) -> p m h x", x=HD)
            ch.mark(v.tensor_tensor(qs, q, q, ALU.mult))
            ch.link(v.tensor_tensor(cq2, c, c, ALU.mult))
            ch.mark(v.reduce_sum(qss, qs, axis=X))
            ch.link(v.reduce_sum(css, cq2, axis=X))
            v.tensor_scalar(stat[:, 0:44], stat[:, 0:44], 1.0 / HD, EPS, ALU.mult, ALU.add).then_inc(s["qk2_mean"], 1)
            v.wait_ge(s["lam_exp"], 1)
            ch.link(v.tensor_tensor(lams[:, 2:3], lams[:, 1:2], lams[:, 0:1], ALU.subtract))
            ch.link(v.tensor_scalar(lams[:, 2:3], lams[:, 2:3], -0.2, None, ALU.add))
            v.wait_ge(s["qk2_root"], 1)
            ch.link(v.reciprocal(stat[:, 0:44], stat[:, 0:44]))
            for m in range(NX):
                ch.mark(v.tensor_tensor(q[:, m], q[:, m], bc(qss[:, m, :], [P, 10, HD], 2), ALU.mult))
            for m in range(NCC):
                ch.mark(v.tensor_tensor(c[:, m], c[:, m], bc(css[:, m, :], [P, 2, HD], 2), ALU.mult))
            ch.wait()
            for m in range(NX):
                ch.mark(v.tensor_tensor(q[:, m, 0:8], q[:, m, 0:8], bc(qkw[:, 0, :], [P, 8, HD], 1), ALU.mult))
                ch.mark(v.tensor_tensor(q[:, m, 8:10], q[:, m, 8:10], bc(qkw[:, 1, :], [P, 2, HD], 1), ALU.mult))
            for m in range(NCC):
                ch.mark(v.tensor_tensor(c[:, m], c[:, m], bc(qkw[:, 1, :], [P, 2, HD], 1), ALU.mult))
            ch.wait()
            v.sem_inc(s["normed2"], 1)
            rotate(v, ch, 0, (0, 1))
            heads_out(v, 0, lambda o, i: v.tensor_copy(o, i), "heads_dve")

        def rotate(eng, ch, j, tiles):
            a, b = rtmp[2 * j], rtmp[2 * j + 1]
            for m in tiles:
                i = raw[:, m, :].rearrange("p (h x two) -> p h x two", h=NH, two=2)
                o = roped[:, m, :].rearrange("p (h x two) -> p h x two", h=NH, two=2)
                co, si = (bc(cs[:, q, m, :], [P, NH, 32], 1) for q in range(2))
                x0, x1 = i[:, :, :, 0], i[:, :, :, 1]
                ch.mark(eng.tensor_tensor(a, x0, co, ALU.mult))
                ch.link(eng.tensor_tensor(b, x1, si, ALU.mult))
                ch.link(eng.tensor_tensor(o[:, :, :, 0], a, b, ALU.subtract))
                ch.mark(eng.tensor_tensor(a, x0, si, ALU.mult))
                ch.link(eng.tensor_tensor(b, x1, co, ALU.mult))
                ch.link(eng.tensor_tensor(o[:, :, :, 1], a, b, ALU.add))
            eng.sem_inc(s["rotated"], 1)

        def pool_rope(g, ch):
            g.wait_ge(s["normed2"], 1)
            rotate(g, ch, 1, (2, 3))

        PAIRS = ([(64 * h, 64 * h + 64) for h in (0, 2, 4, 6)]
                 + [(1024 + 128 * h, 1088 + 128 * h) for h in range(4)]
                 + [(512 + 64 * h, 512 + 64 * h + 64) for h in (0, 2, 4, 6)] + [(1536, 1600)])

        def pe_heads(pe):
            pe.wait_ge(s["rotated"], 2)
            for n, (c0, c1) in enumerate(PAIRS):
                lat, cx = (n % 4), 4 + n % 4
                if n >= 4:
                    sem = "heads_dve" if n % 2 == 0 else "heads_act"
                    pe.wait_ge(s[sem], (n - 4) // 2 + 1)
                for m in range(NX):
                    src = roped[:, m, c0:c1 + 64]
                    last = pe.transpose(ps[:, lat, m * P:(m + 1) * P], src, ident[:, :])
                if n >= 8:
                    k0 = c0 - 512 if c0 < 1024 else 512
                    for m in range(NCC):
                        last = pe.transpose(ps[:, cx, m * P:(m + 1) * P], ctk[:, m, k0:k0 + P], ident[:, :])
                last.then_inc(s["heads_ps"], 1)

        def heads_out(eng, mine, copy, sem):
            eng.wait_ge(s["rotated"], 2)
            for n in range(len(PAIRS)):
                if n % 2 != mine:
                    continue
                eng.wait_ge(s["heads_ps"], n + 1)
                if n < 8:
                    last = copy(aQT[:, n, :], ps[:, n % 4, :])
                else:
                    copy(aKT[:, n - 8, CTX:], ps[:, n % 4, :])
                    last = copy(aKT[:, n - 8, 0:CTX], ps[:, 4 + n % 4, 0:CTX])
                last.then_inc(s[sem], 1)

        Pm = [at(18688 + 1536 * b, 2, TOK) for b in range(2)]
        PT = at(21760, 12, P)
        oat = at(6656, NX, D)
        asm = bet[:, 0:2, :]
        AU = 32
        SC = HD ** -0.5

        def aunit(u):
            return u // 16, (u // 4) % 4, u % 4

        def pe_attn(pe):
            def scores(u):
                g, h, m = aunit(u)
                if u:
                    pe.wait_ge(s["exp_done"], u)
                for a in range(2):
                    if g:
                        q, k, r = aQT[:, 4 + h, :], aKT[:, 4, :], a
                    else:
                        q, k, r = aQT[:, 2 * a + h // 2, :], aKT[:, 2 * a + h // 2, :], h % 2
                    q, k = q[64 * r:64 * r + 64], k[64 * r:64 * r + 64]
                    pe.matmul(ps[:, 2 * a, :], q[:, m * P:(m + 1) * P], k[:, 0:BANK], start=True, stop=True)
                    last = pe.matmul(ps[:, 2 * a + 1, 0:TOK - BANK], q[:, m * P:(m + 1) * P], k[:, BANK:TOK], start=True, stop=True)
                last.then_inc(s["score2_ps"], 1)

            def values(u):
                g, h, m = aunit(u)
                n = 12 if g else 6
                pe.wait_ge(s["probs_ready"], u + 1)
                if u:
                    pe.wait_ge(s["pt_act"], u)
                    pe.wait_ge(s["pt_dve"], u)
                p = Pm[u % 2].rearrange("p a t -> p (a t)")
                for j in range(n):
                    last = pe.transpose(ps[:, 4 + j // 4, (j % 4) * P:(j % 4 + 1) * P], p[:, j * P:(j + 1) * P], ident[:, :])
                last.then_inc(s["pt_ps"], 1)
                pe.wait_ge(s["pt_act"], u + 1)
                pe.wait_ge(s["pt_dve"], u + 1)
                if u:
                    pe.wait_ge(s["att_out"], u)
                if not g:
                    for j in range(NC):
                        last = pe.matmul(ps[:, 7, 0:P], PT[:, j, :], V[:, j, h * P:(h + 1) * P], start=(j == 0), stop=(j == NC - 1))
                else:
                    for a in range(2):
                        for j in range(NC):
                            last = pe.matmul(ps[:, 7, a * HD:(a + 1) * HD], PT[:, 6 * a + j, :],
                                             V[:, j, 512 + a * HD:512 + (a + 1) * HD], start=(j == 0), stop=(j == NC - 1))
                last.then_inc(s["att_ps"], 1)

            scores(0)
            for u in range(AU):
                if u + 1 < AU:
                    scores(u + 1)
                values(u)

        def act_attn(a):
            for u in range(AU + 1):
                if u < AU:
                    a.wait_ge(s["negmax"], u + 1)
                    if u >= 2:
                        a.wait_ge(s["pt_ps"], u - 1)
                    for q in range(2):
                        last = a.activation(Pm[u % 2][:, q, :], ps[:, 2 * q:2 * q + 2, :].rearrange("p a b -> p (a b)")[:, 0:TOK],
                                            ACT.Exp, bias=asm[:, u % 2, 2 + q:3 + q], scale=SC,
                                            accum_out=asm[:, u % 2, 4 + q:5 + q])
                    last.then_inc(s["exp_done"], 1)
                if u >= 1:
                    g = (u - 1) // 16
                    a.wait_ge(s["pt_ps"], u)
                    if u >= 2:
                        a.wait_ge(s["att_ps"], u - 1)
                    last = a.activation(PT[:, 0:4, :].rearrange("p a b -> p (a b)"), ps[:, 4, :], ACT.Copy)
                    if g:
                        last = a.activation(PT[:, 8:12, :].rearrange("p a b -> p (a b)"), ps[:, 6, :], ACT.Copy)
                    last.then_inc(s["pt_act"], 1)

        def dve_attn(v, ch):
            for u in range(AU + 1):
                if u < AU:
                    g = u // 16
                    t = asm[:, u % 2, :]
                    v.wait_ge(s["score2_ps"], u + 1)
                    if u >= 2:
                        v.wait_ge(s["att_out"], u - 1)
                    mp = ps[:, 0:4, :].rearrange("p (a b) c -> p a (b c)", a=2)[:, :, 0:TOK]
                    ch.link(v.reduce_max(t[:, 0:2], mp, axis=X))
                    v.tensor_scalar(t[:, 2:4], t[:, 0:2], -SC, None, ALU.mult).then_inc(s["negmax"], 1)
                if u >= 1:
                    w = u - 1
                    g, h, m = aunit(w)
                    v.wait_ge(s["pt_ps"], w + 1)
                    if w:
                        v.wait_ge(s["att_ps"], w)
                    n = 512 if g else 256
                    v.tensor_copy(PT[:, 4:4 + n // P, :].rearrange("p a b -> p (a b)"), ps[:, 5, 0:n]).then_inc(s["pt_dve"], 1)
                if u < AU:
                    g = u // 16
                    v.wait_ge(s["exp_done"], u + 1)
                    ch.link(v.reciprocal(t[:, 6:8], t[:, 4:6]))
                    if not g:
                        pm = Pm[u % 2]
                        ch.mark(v.tensor_scalar(pm[:, 0, :], pm[:, 0, :], t[:, 6:7], None, ALU.mult))
                        ch.link(v.tensor_tensor(t[:, 7:8], t[:, 7:8], lams[:, 2:3], ALU.mult))
                        ch.link(v.scalar_tensor_tensor(out=pm[:, 0, :], in0=pm[:, 1, :], scalar=t[:, 7:8], in1=pm[:, 0, :],
                                                       op0=ALU.mult, op1=ALU.add))
                    v.sem_inc(s["probs_ready"], 1)
                if u >= 1:
                    w = u - 1
                    g, h, m = aunit(w)
                    tw = asm[:, w % 2, :]
                    v.wait_ge(s["att_ps"], w + 1)
                    if not g:
                        last = v.tensor_copy(oat[:, m, h * P:(h + 1) * P], ps[:, 7, 0:P])
                    else:
                        for a in range(2):
                            c0 = 512 + (h + 4 * a) * HD
                            last = v.tensor_scalar(oat[:, m, c0:c0 + HD], ps[:, 7, a * HD:(a + 1) * HD], tw[:, 6 + a:7 + a], None, ALU.mult)
                    last.then_inc(s["att_out"], 1)

        ao_sq = at(10752, NX, 4, P)
        ass = stat[:, 0:16]
        fits = stat[:, 16:32]
        SMALL = 2.0 ** -40
        FMAX = 3.4028234663852886e38

        def act_awout(a):
            a.wait_ge(s["sub_mean"], 1)
            a.activation(ass, ass, ACT.Sqrt).then_inc(s["sub_root"], 1)
            act_transpose_out(a)

        def dve_awout(v, ch):
            for m in range(NX):
                ch.mark(v.tensor_scalar(oat[:, m, 0:512], oat[:, m, 0:512], SMALL, None, ALU.mult))
            ch.wait()
            for m in range(NX):
                o = oat[:, m, 0:512].rearrange("p (h x) -> p h x", x=P)
                ch.mark(v.tensor_tensor(ao_sq[:, m], o, o, ALU.mult))
            ch.wait()
            ch.link(v.reduce_sum(ass, ao_sq.rearrange("p m h x -> p (m h) x"), axis=X))
            ch.link(v.tensor_scalar(fits, ass, FMAX * SMALL * SMALL, 0.8, ALU.is_le, ALU.mult))
            v.tensor_scalar(ass, ass, 1.0 / P, EPS * SMALL * SMALL, ALU.mult, ALU.add).then_inc(s["sub_mean"], 1)
            v.wait_ge(s["sub_root"], 1)
            ch.link(v.reciprocal(ass, ass))
            ch.link(v.tensor_tensor(ass, ass, fits, ALU.mult))
            for m in range(NX):
                o = oat[:, m, 0:512].rearrange("p (h x) -> p h x", x=P)
                ch.mark(v.tensor_tensor(o, o, bc(ass[:, 4 * m:4 * m + 4], [P, 4, P], 2), ALU.mult))
            ch.wait()
            for m in range(NX):
                o = oat[:, m, 0:512].rearrange("p (h x) -> p h x", x=P)
                last = v.tensor_tensor(o, o, bc(subw[:, :], [P, 4, P], 1), ALU.mult)
            last.then_inc(s["srcT_ready"], 1)
            dve_transpose_out(v)
            dve_out(v, wo_tmp2)

        wo_tmp2 = at(12800, TP, CW)

        fa = at(4096, NF, SEQ)
        NZ = 4
        zg = at(4096 + NF * SEQ, NZ, SEQ)
        zu = at(4096 + NF * SEQ + NZ * SEQ, NZ, SEQ)
        ftmp = at(4096 + NF * SEQ, TP, BANK)
        NPAIR = NF // 2

        def sp_ffn(W, l):
            up = ins["ffn_w_up_2"][l].rearrange("(k p) n -> p k n", p=P)
            for jj in range(NPAIR):
                W.load(cols_of(up, jj * CW))
                W.load(cols_of(up, FFN + jj * CW))
            dn = ins["ffn_w_down_2"][l].rearrange("(f p) n -> p f n", p=P)
            for half in range(2):
                for q in range(0, NF, 4):
                    n = min(4, NF - q)
                    W.load(dn[:, q:q + n, half * 512:(half + 1) * 512], n * 512)

        def pe_ffn(pe, W, l):
            pe_norm(pe, NX, xn_buf)
            pe.wait_ge(s["h2_act"], MOE + 1 + l)
            pe.wait_ge(s["h2_dve"], MOE + 1 + l)
            n0 = 4 * NPAIR * l
            f = 0
            for jj in range(NPAIR):
                for kind in range(2):
                    w = W.take(KD)
                    for j in range(2):
                        if f >= 8:
                            pe.wait_ge(s["conv_out"], n0 + f - 7)
                        for k in range(KD):
                            last = pe.matmul(ps[:, f % 8, :], w[:, k, j * P:(j + 1) * P], hT[:, k, :],
                                             start=(k == 0), stop=(k == KD - 1))
                            if k == 0:
                                W.pay(last)
                        last.then_inc(s["up_ps"], 1)
                        f += 1
                    W.done()
            pe.wait_ge(s["conv_out"], n0 + 4 * NPAIR)
            for half in range(2):
                for q in range(0, NF, 4):
                    n = min(4, NF - q)
                    w = W.take(n, n * 512)
                    for k in range(n):
                        if half == 0:
                            pe.wait_ge(s["fa_ready"], NF * l + q + k + 1)
                        for m in range(NX):
                            last = pe.matmul(ps[:, 4 * half + m, :], fa[:, q + k, m * P:(m + 1) * P], w[:, k, :],
                                             start=(q + k == 0), stop=(q + k == NF - 1))
                            if k == 0 and m == 0:
                                W.pay(last)
                    if q + n < NF:
                        W.done()
                last.then_inc(s["down_ps"], 1)
                W.done()
            W.pay()

        def ffn_units():
            return [(2 * jj + j, kind) for jj in range(NPAIR) for kind in range(2) for j in range(2)]

        def act_ffn(a, ch, l):
            act_norm(a, xres, NX, njunk, hT, 1, 0, xn_buf, stat[:, 0:4], 2 * KD)
            a.drain().then_inc(s["h2_act"], 1)
            n0 = 4 * NPAIR * l
            for f, (j, kind) in enumerate(ffn_units()):
                z = (zu if kind else zg)[:, j % NZ, :]
                t = j + NF * kind
                a.wait_ge(s["up_ps"], n0 + f + 1)
                if j >= NZ:
                    a.wait_ge(s["fa_ready"], NF * l + j - NZ + 1)
                a.activation(z, ps[:, f % 8, :], ACT.Identity, bias=col(4 + 2 * l, 2 * NF + t),
                             scale=col(3 + 2 * l, 2 * NF + t)).then_inc(s["mid_tap"], 1)
                if kind == 1 and j % 2 == 1:
                    for jj in (j - 1, j):
                        a.wait_ge(s["conv_out"], n0 + 4 * (j // 2) + 1 + jj % 2)
                        if jj >= NZ:
                            pass
                        a.activation(zg[:, jj % NZ, :], zg[:, jj % NZ, :], ACT.Silu).then_inc(s["zg_silu"], 1)

        def dve_ffn(v, ch, l):
            dve_norm(v, ch, xres, NX, hT, 1, 0, xn_buf, stat[:, 0:4], 2 * KD)
            v.drain().then_inc(s["h2_dve"], 1)
            n0 = 4 * NPAIR * l
            for f, (j, kind) in enumerate(ffn_units()):
                z = (zu if kind else zg)[:, j % NZ, :]
                t = j + NF * kind
                v.wait_ge(s["mid_tap"], n0 + f + 1)
                ch.link(v.scalar_tensor_tensor(out=z[:, 1:SEQ], in0=ps[:, f % 8, 0:SEQ - 1], scalar=col(3 + 2 * l, t),
                                               in1=z[:, 1:SEQ], op0=ALU.mult, op1=ALU.add))
                v.scalar_tensor_tensor(out=z[:, 0:SEQ - 1], in0=ps[:, f % 8, 1:SEQ], scalar=col(4 + 2 * l, t),
                                       in1=z[:, 0:SEQ - 1], op0=ALU.mult, op1=ALU.add).then_inc(s["conv_out"], 1)
            for half in range(2):
                v.wait_ge(s["down_ps"], 2 * l + half + 1)
                v.wait_ge(s["fa_ready"], NF * (l + 1))
                for m in range(NX):
                    if half:
                        v.wait_ge(s["fadded"], 8 * l + m + 1)
                    v.tensor_tensor(ftmp[:, m, :], ps[:, 4 * half + m, :], gate[:, 1, half * 512:(half + 1) * 512],
                                    ALU.mult).then_inc(s["fgated"], 1)

        def pool_ffn(g, l):
            n0 = 4 * NPAIR * l
            for j in range(NF):
                g.wait_ge(s["zg_silu"], NF * l + j + 1)
                g.wait_ge(s["conv_out"], n0 + 4 * (j // 2) + 3 + j % 2)
                g.tensor_tensor(fa[:, j, :], zg[:, j % NZ, :], zu[:, j % NZ, :], ALU.mult).then_inc(s["fa_ready"], 1)
            for u in range(8):
                half, m = divmod(u, 4)
                g.wait_ge(s["fgated"], 8 * l + u + 1)
                x = xres[:, m, half * 512:(half + 1) * 512]
                g.tensor_tensor(x, x, ftmp[:, m, :], ALU.add).then_inc(s["fadded"], 1)

        zs = at(0, NX, 2 * D)
        so = at(8192, NX, D)
        ws = at(12288, 4, P)
        wsT = at(12800, 4, P)
        vw = at(13312, D)
        ssq = at(14336, NX, D)
        wo_tmp3 = at(18432, TP, CW)

        def sp_sgu(sp, W):
            v = ins["sgu_w_in_2"][0].rearrange("(k p) n -> p k n", p=P)
            for q in range(8):
                W.load(cols_of(v, q * CW))
            sp.wait_ge(s["stage_done"], 4 * (STAGES.index("norm3") + 1 - len(skip)))
            sp.dma_start(ws[:, :, :], ins["sgu_w_s_2"][0].rearrange("g p q -> p g q")).then_inc(s["sgu_in"], 16)
            sp.dma_start(vw[:, :], ins["sgu_v_norm_2"].broadcast_to([P, D])).then_inc(s["sgu_in"], 16)

        def pe_sgu(pe, W):
            for q in range(8):
                w = W.take(KD)
                for m in range(NX):
                    u = 4 * q + m
                    if u >= 8:
                        pe.wait_ge(s["gelu_out"], u - 7)
                    for k in range(KD):
                        last = pe.matmul(ps[:, u % 8, 0:CW], hT[:, k, m * P:(m + 1) * P], w[:, k, :],
                                         start=(k == 0), stop=(k == KD - 1))
                        if k == 0:
                            W.pay(last)
                    last.then_inc(s["zs_ps"], 1)
                W.done()
            W.pay()
            pe.wait_ge(s["sgu_in"], 32)
            pe.wait_ge(s["gelu_out"], 32)
            for g in range(4):
                last = pe.transpose(ps[:, 0, g * P:(g + 1) * P], ws[:, g, :], ident[:, :])
            last.then_inc(s["wsT_ps"], 1)
            pe.wait_ge(s["v_ready"], 1)
            for m in range(NX):
                for g in range(4):
                    last = pe.matmul(ps[:, 2 * m + g // 2, (g % 2) * CW:(g % 2 + 1) * CW], wsT[:, g, :],
                                     zs[:, m, D + g * CW:D + (g + 1) * CW], start=True, stop=True)
                last.then_inc(s["mix_ps"], 1)

        def act_sgu(a):
            for u in range(32):
                q, m = divmod(u, 4)
                a.wait_ge(s["zs_ps"], u + 1)
                a.activation(zs[:, m, q * CW:(q + 1) * CW], ps[:, u % 8, 0:CW], ACT.Gelu).then_inc(s["gelu_out"], 1)
            a.wait_ge(s["gelu_out"], 32)
            for m in range(NX):
                last = a.activation(ssq[:, m, :], zs[:, m, D:], ACT.Square, accum_out=stat[:, m:m + 1])
            last.then_inc(s["v_sumsq"], 1)
            a.wait_ge(s["v_mean"], 1)
            a.activation(stat[:, 0:4], stat[:, 0:4], ACT.Sqrt).then_inc(s["v_root"], 1)

        def dve_sgu(v, ch):
            v.wait_ge(s["wsT_ps"], 1)
            ch.mark(v.tensor_copy(wsT[:, :, :].rearrange("p a b -> p (a b)"), ps[:, 0, :]))
            v.wait_ge(s["v_sumsq"], 1)
            v.tensor_scalar(stat[:, 0:4], stat[:, 0:4], 1.0 / D, EPS, ALU.mult, ALU.add).then_inc(s["v_mean"], 1)
            v.wait_ge(s["v_root"], 1)
            ch.link(v.reciprocal(stat[:, 0:4], stat[:, 0:4]))
            for m in range(NX):
                last = v.scalar_tensor_tensor(out=zs[:, m, D:], in0=zs[:, m, D:], scalar=stat[:, m:m + 1], in1=vw[:, :],
                                              op0=ALU.mult, op1=ALU.mult)
            last.then_inc(s["v_ready"], 1)
            for m in range(NX):
                v.wait_ge(s["mix_ps"], m + 1)
                for g in range(4):
                    last = v.scalar_tensor_tensor(out=so[:, m, g * CW:(g + 1) * CW],
                                                  in0=ps[:, 2 * m + g // 2, (g % 2) * CW:(g % 2 + 1) * CW],
                                                  scalar=col(1, 96 + g), in1=zs[:, m, g * CW:(g + 1) * CW],
                                                  op0=ALU.add, op1=ALU.mult)
            last.then_inc(s["srcT_ready"], 1)

        block = ctx.enter_context(nc.Block())

        @block.sync
        def _(sp):
            W = Stream(sp)
            sp_consts(sp)
            for m in range(NX):
                sp.dma_start(xres[:, m, :], ins["x"][0, m * P:(m + 1) * P, :]).then_inc(s["x_in"], 16)
            if on("mod1"):
                sp_mod(sp, W, 0)
            if on("hg0"):
                sp_hg(sp, W, 0)
            if on("hg1"):
                sp_hg(sp, W, 1)
            if on("dn0"):
                sp_dn(sp, W, 0)
            if on("dn1"):
                sp_dn(sp, W, 1)
            if on("wout"):
                sp_out(W, ins["w_out"][0])
            if on("moe"):
                sp_router(sp)
                sp_moe(sp, W)
            if on("mod2"):
                sp_mod(sp, W, 1)
            if on("proj"):
                sp_proj(sp, W)
            if on("awout"):
                sp_out(W, ins["attn_w_out_2"][0])
            if on("ffn0"):
                sp_ffn(W, 0)
            if on("mod3"):
                sp_mod(sp, W, 2)
            if on("sgu"):
                sp_sgu(sp, W)
            if on("sguout"):
                sp_out(W, ins["sgu_w_out_2"][0])
            if on("ffn1"):
                sp_ffn(W, 1)
            if on("final"):
                for m in range(NX):
                    sp.wait_ge(s["final_ready"], 4 * MOE + 1 + m)
                    sp.dma_start(out[0, m * P:(m + 1) * P, :], xres[:, m, :]).then_inc(s["y_out"], 16)
                sp.wait_ge(s["y_out"], 64)
            if dbg is not None:
                sp.wait_ge(s["stage_done"], 4 * (upto - len(skip)))
                nd = {"hg0": 256, "hg1": 512}.get(stop, 1024)
                n0 = 512 if "hg0" in skip and stop in ("dn0", "dn1") else 0
                sp.dma_start(dbg["arena"].rearrange("p (a b) -> p a b", b=1024)[:, :, n0:nd], at(6656 if stop in ("attn", "awout") else 0, 4, 1024)[:, :, n0:nd]).then_inc(s["out_sent"], 16)
                sp.dma_start(dbg["hT"], hT[:, :, :]).then_inc(s["out_sent"], 16)
                sp.dma_start(dbg["hcT"], hcT[:, :, :]).then_inc(s["out_sent"], 16)
                sp.dma_start(dbg["xres"][:, :, n0:], xres[:, :, n0:]).then_inc(s["out_sent"], 16)
                sp.wait_ge(s["out_sent"], 64)

        @block.tensor
        def _(pe):
            W = Stream(pe)
            pe_consts(pe)
            meet(pe, "pe")
            if on("mod1"):
                pe_mod(pe, W, 0)
                meet(pe, "pe")
            if on("norm1"):
                pe_norm(pe, NX, xn_buf)
                pe.wait_ge(s["hT_out"], 1)
                pe.wait_ge(s["hT_out2"], 1)
                pe_norm(pe, NCC, xn_buf)
                meet(pe, "pe")
            for p in range(2):
                if on(f"hg{p}"):
                    pe_hg(pe, W, p)
                    meet(pe, "pe")
            for p in range(2):
                if on(f"dn{p}"):
                    pe_dn(pe, W, p)
                    meet(pe, "pe")
            if on("wout"):
                pe_wout(pe, W)
                meet(pe, "pe")
            if on("moe"):
                pe_moe(pe, W)
                meet(pe, "pe")
            if on("mod2"):
                pe_mod(pe, W, 1)
                meet(pe, "pe")
            if on("norm2"):
                pe_norm(pe, NX, xn_buf)
                pe.wait_ge(s["hT_out"], 2)
                pe.wait_ge(s["hT_out2"], 2)
                pe_norm(pe, NCC, xn_buf)
                meet(pe, "pe")
            if on("proj"):
                pe_aproj(pe, W)
                meet(pe, "pe")
            if on("rope"):
                pe_heads(pe)
                meet(pe, "pe")
            if on("attn"):
                pe_attn(pe)
                meet(pe, "pe")
            if on("awout"):
                pe_transpose_in(pe, oat, NX)
                pe_out(pe, W)
                meet(pe, "pe")
            if on("ffn0"):
                pe_ffn(pe, W, 0)
                meet(pe, "pe")
            if on("mod3"):
                pe_mod(pe, W, 2)
                meet(pe, "pe")
            if on("norm3"):
                pe_norm(pe, NX, xn_buf)
                meet(pe, "pe")
            if on("sgu"):
                pe_sgu(pe, W)
                meet(pe, "pe")
            if on("sguout"):
                pe_transpose_in(pe, so, NX)
                pe_out(pe, W)
                meet(pe, "pe")
            if on("ffn1"):
                pe_ffn(pe, W, 1)
                meet(pe, "pe")
            if on("final"):
                pass
                meet(pe, "pe")

        @block.scalar
        def _(a):
            ch = Chain(a, "act_steps")
            meet(a, "act")
            if on("mod1"):
                for m in range(NCC):
                    a.dma_start(cres[:, m, :], ins["ctx"][0, m * P:(m + 1) * P, :]).then_inc(s["ctx_in"], 16)
                act_mod(a, ch, 0)
                meet(a, "act")
            if on("norm1"):
                a.wait_ge(s["x_in"], 64)
                act_norm(a, xres, NX, njunk, hT, 0, 0, xn_buf, stat[:, 0:4], 0)
                a.drain().then_inc(s["hT_out"], 1)
                a.wait_ge(s["ctx_in"], 32)
                act_norm(a, cres, NCC, njunk, hcT, 0, 1, xn_buf, stat[:, 4:6], 0)
                meet(a, "act")
            for p in range(2):
                if on(f"hg{p}"):
                    act_hg(a, p)
                    meet(a, "act")
            for p in range(2):
                if on(f"dn{p}"):
                    act_dn(a, ch, p)
                    meet(a, "act")
            if on("wout"):
                act_wout(a)
                meet(a, "act")
            if on("moe"):
                act_moe(a)
                act_final(a, 0, ins["final_norm_w"])
                meet(a, "act")
            if on("mod2"):
                for m in range(NCC):
                    a.dma_start(cres[:, m, :], ins["ctx_2"][0, m * P:(m + 1) * P, :]).then_inc(s["ctx_in"], 16)
                act_mod(a, ch, 1)
                meet(a, "act")
            if on("norm2"):
                act_norm(a, xres, NX, njunk, hT, 0, 0, xn_buf, stat[:, 0:4], 0)
                a.drain().then_inc(s["hT_out"], 1)
                a.wait_ge(s["ctx_in"], 64)
                act_norm(a, cres, NCC, njunk, hcT, 0, 1, xn_buf, stat[:, 4:6], 0)
                meet(a, "act")
            if on("proj"):
                aproj_out(a, 0, lambda o, i: a.activation(o, i, ACT.Copy), "ap_act")
                meet(a, "act")
            if on("rope"):
                act_rope(a, ch)
                meet(a, "act")
            if on("attn"):
                act_attn(a)
                meet(a, "act")
            if on("awout"):
                act_awout(a)
                meet(a, "act")
            if on("ffn0"):
                act_ffn(a, ch, 0)
                meet(a, "act")
            if on("mod3"):
                act_mod(a, ch, 2)
                meet(a, "act")
            if on("norm3"):
                act_norm(a, xres, NX, njunk, hT, 0, 0, xn_buf, stat[:, 0:4], 0)
                meet(a, "act")
            if on("sgu"):
                act_sgu(a)
                meet(a, "act")
            if on("sguout"):
                act_transpose_out(a)
                meet(a, "act")
            if on("ffn1"):
                act_ffn(a, ch, 1)
                meet(a, "act")
            if on("final"):
                act_final(a, 1, ins["final_norm_2"])
                meet(a, "act")

        @block.vector
        def _(v):
            ch = Chain(v, "dve_steps")
            dve_consts(v)
            meet(v, "dve")
            if on("mod1"):
                dve_mod(v, ch, 0, [col(0, 32, 8), col(0, 40, 8)], 1)
                meet(v, "dve")
            if on("norm1"):
                v.wait_ge(s["x_in"], 64)
                dve_norm(v, ch, xres, NX, hT, 0, 0, xn_buf, stat[:, 0:4], 0)
                v.drain().then_inc(s["hT_out2"], 1)
                v.wait_ge(s["ctx_in"], 32)
                dve_norm(v, ch, cres, NCC, hcT, 0, 1, xn_buf, stat[:, 4:6], 0)
                meet(v, "dve")
            for p in range(2):
                if on(f"hg{p}"):
                    dve_hg(v, ch, p)
                    meet(v, "dve")
            for p in range(2):
                if on(f"dn{p}"):
                    dve_dn(v, ch, p)
                    meet(v, "dve")
            if on("wout"):
                dve_wout(v, ch)
                meet(v, "dve")
            if on("moe"):
                dve_moe(v, ch)
                dve_final(v, ch, 0)
                meet(v, "dve")
            if on("mod2"):
                dve_mod(v, ch, 1, [col(0, 48, 8), col(0, 64, 8)], 2)
                meet(v, "dve")
            if on("norm2"):
                dve_norm(v, ch, xres, NX, hT, 0, 0, xn_buf, stat[:, 0:4], 0)
                v.drain().then_inc(s["hT_out2"], 1)
                v.wait_ge(s["ctx_in"], 64)
                dve_norm(v, ch, cres, NCC, hcT, 0, 1, xn_buf, stat[:, 4:6], 0)
                meet(v, "dve")
            if on("proj"):
                aproj_out(v, 1, lambda o, i: v.tensor_copy(o, i), "ap_dve")
                meet(v, "dve")
            if on("rope"):
                dve_rope(v, ch)
                meet(v, "dve")
            if on("attn"):
                dve_attn(v, ch)
                meet(v, "dve")
            if on("awout"):
                dve_awout(v, ch)
                meet(v, "dve")
            if on("ffn0"):
                dve_ffn(v, ch, 0)
                meet(v, "dve")
            if on("mod3"):
                dve_mod(v, ch, 2, [col(0, 56, 8), col(0, 72, 8)], 3)
                meet(v, "dve")
            if on("norm3"):
                dve_norm(v, ch, xres, NX, hT, 0, 0, xn_buf, stat[:, 0:4], 0)
                meet(v, "dve")
            if on("sgu"):
                dve_sgu(v, ch)
                meet(v, "dve")
            if on("sguout"):
                dve_transpose_out(v)
                dve_out(v, wo_tmp3)
                meet(v, "dve")
            if on("ffn1"):
                dve_ffn(v, ch, 1)
                meet(v, "dve")
            if on("final"):
                v.sem_inc(s["x_done"], 1)
                dve_final(v, ch, 1)
                meet(v, "dve")

        @block.gpsimd
        def _(g):
            ch = Chain(g, "pool_steps")
            pool_consts(g, ch)
            meet(g, "pool")
            if on("mod1"):
                meet(g, "pool")
            if on("norm1"):
                meet(g, "pool")
            for p in range(2):
                if on(f"hg{p}"):
                    pool_hg(g, ch, p)
                    meet(g, "pool")
            for p in range(2):
                if on(f"dn{p}"):
                    pool_dn(g, ch, p)
                    meet(g, "pool")
            if on("wout"):
                pool_wout(g)
                meet(g, "pool")
            if on("moe"):
                pass
                meet(g, "pool")
            if on("mod2"):
                pass
                meet(g, "pool")
            if on("norm2"):
                pass
                meet(g, "pool")
            if on("proj"):
                pass
                meet(g, "pool")
            if on("rope"):
                pool_rope(g, ch)
                meet(g, "pool")
            if on("attn"):
                pass
                meet(g, "pool")
            if on("awout"):
                pool_out(g, wo_tmp2)
                meet(g, "pool")
            if on("ffn0"):
                pool_ffn(g, 0)
                meet(g, "pool")
            if on("mod3"):
                pass
                meet(g, "pool")
            if on("norm3"):
                pass
                meet(g, "pool")
            if on("sgu"):
                pass
                meet(g, "pool")
            if on("sguout"):
                pool_out(g, wo_tmp3)
                meet(g, "pool")
            if on("ffn1"):
                pool_ffn(g, 1)
                meet(g, "pool")
            if on("final"):
                pass
                meet(g, "pool")


N_OUT = (1, SEQ, D)


def rope_table():
    import numpy as np
    f = np.float32
    n = 16
    inv = f(10000.0) ** (-np.arange(n, dtype=f) / f(n))
    row = np.repeat(np.arange(GRID_R, dtype=f), GRID_W)
    col = np.tile(np.arange(GRID_W, dtype=f), GRID_R)
    ang = np.concatenate([row[:, None] * inv, col[:, None] * inv], axis=-1)
    return np.stack([np.cos(ang), np.sin(ang)]).astype(f)


def kernel(**inputs):
    import numpy as np
    import concourse.bacc as bacc
    from concourse.bass_utils import run_bass_kernel_spmd

    nc = bacc.Bacc("TRN2", target_bir_lowering=False, num_devices=1)
    arrays, ins = {}, {}
    for name, a in list(inputs.items()) + [("rope", rope_table())]:
        a = np.ascontiguousarray(a)
        arrays["in_" + name] = a
        ins[name] = nc.dram_tensor("in_" + name, a.shape, mybir.dt.from_np(a.dtype), kind="ExternalInput").ap()
    out = nc.dram_tensor("out", N_OUT, F32, kind="ExternalOutput").ap()
    build(nc, ins, out)
    r = run_bass_kernel_spmd(nc, [arrays], core_ids=[0])
    return r.results[0]["out"]
```
